# Optimizing a Trainium2 kernel written in Bass

```python
import jax, jax.numpy as jnp
from jax import lax
import numpy as np

D_MODEL = 1024
BATCH = 1
SEQ = 512
DEPTH = 4

N_MIXERS = 3
N_A_LAYERS = (DEPTH + 2) // 3
N_B_LAYERS = (DEPTH + 1) // 3
N_C_LAYERS = DEPTH // 3
NORM_EPS = 1e-6
NEG_BIG = -1e30
LB_FLOOR = 1e-30

A_WIDTH = D_MODEL
A_HEAD_DIM = 128
A_HEADS = A_WIDTH // A_HEAD_DIM
A_CHUNK = 64

B_HEAD_DIM = 64
B_HEADS = D_MODEL // B_HEAD_DIM
B_WIDTH = B_HEADS * B_HEAD_DIM
DILATED_GROUPS = ((128, 1), (512, 4), (2048, 16))
B_N_GROUPS = len(DILATED_GROUPS)
ALIBI_MAX_EXP = 8.0

C_WIDTH = D_MODEL
C_CHUNK = 128
C_GROUPS = 8
C_GROUP_DIM = C_WIDTH // C_GROUPS

kernel_name = 'hybrid_hgrn2_dilated_gmlp'

def rms_norm(x, w):
    xf = x.astype(jnp.float32)
    y = xf * lax.rsqrt(jnp.mean(xf * xf, axis=-1, keepdims=True) + NORM_EPS)
    return (y * w.astype(jnp.float32)).astype(x.dtype)

def layer_norm(x, w, b):
    xf = x.astype(jnp.float32)
    mu = jnp.mean(xf, axis=-1, keepdims=True)
    xc = xf - mu
    y = xc * lax.rsqrt(jnp.mean(xc * xc, axis=-1, keepdims=True) + NORM_EPS)
    return (y * w.astype(jnp.float32) + b.astype(jnp.float32)).astype(x.dtype)

def hgrn2_mixer(h, w_in, lower_bound, o_norm_w, w_out):
    bsz, seq, _ = h.shape
    n_chunks = seq // A_CHUNK
    q, f, inp_v, g = jnp.split(h @ w_in, 4, axis=-1)
    f32 = jnp.float32
    q = jax.nn.silu(q.astype(f32))
    f = f.astype(f32)
    lb = lower_bound.astype(f32)
    k = (1.0 - lb) * jax.nn.sigmoid(-f)
    log_f = jnp.logaddexp(jnp.log(jnp.maximum(lb, LB_FLOOR)),
                          jnp.log1p(-lb) + jax.nn.log_sigmoid(f))

    def heads(t):
        return t.reshape(bsz, n_chunks, A_CHUNK, A_HEADS, A_HEAD_DIM).transpose(1, 0, 3, 2, 4)

    xs = (heads(q), heads(k), heads(inp_v.astype(f32)), heads(log_f))
    causal = jnp.tril(jnp.ones((A_CHUNK, A_CHUNK), dtype=bool))

    def chunk_step(state, inp):
        qc, kc, vc, lc = inp
        b = jnp.cumsum(lc, axis=-2)
        diff = b[..., :, None, :] - b[..., None, :, :]
        decay = jnp.exp(jnp.where(causal[:, :, None], diff, NEG_BIG))
        scores = jnp.einsum('bhtk,bhsk,bhtsk->bhts', qc, kc, decay)
        o = scores @ vc + jnp.einsum('bhtk,bhkv->bhtv', qc * jnp.exp(b), state)
        b_last = b[..., -1:, :]
        state = (jnp.exp(b_last[..., 0, :])[..., None] * state
                 + jnp.einsum('bhsk,bhsv->bhkv', kc * jnp.exp(b_last - b), vc))
        return state, o

    state0 = jnp.zeros((bsz, A_HEADS, A_HEAD_DIM, A_HEAD_DIM), f32)
    _, o = lax.scan(chunk_step, state0, xs)
    o = o.transpose(1, 0, 3, 2, 4).reshape(bsz, seq, A_HEADS, A_HEAD_DIM)
    o = rms_norm(o, o_norm_w).reshape(bsz, seq, A_WIDTH)
    y = (o * jax.nn.silu(g.astype(f32))).astype(h.dtype)
    return y @ w_out

def dilated_window_attention(q, k, v, window, dilation, slopes):
    bsz, nh, seq, hd = q.shape
    n_keys = window // dilation
    sub_len = seq // dilation
    n_blk = -(-sub_len // n_keys)
    pad = n_blk * n_keys - sub_len

    def to_blocks(t):
        t = t.reshape(bsz, nh, sub_len, dilation, hd).transpose(0, 1, 3, 2, 4)
        t = jnp.pad(t, ((0, 0), (0, 0), (0, 0), (0, pad), (0, 0)))
        return t.reshape(bsz, nh, dilation, n_blk, n_keys, hd)

    def with_prev(t):
        prev = jnp.pad(t, ((0, 0), (0, 0), (0, 0), (1, 0), (0, 0), (0, 0)))[:, :, :, :-1]
        return jnp.concatenate([prev, t], axis=-2)

    qb = to_blocks(q)
    kb = with_prev(to_blocks(k))
    vb = with_prev(to_blocks(v))
    scores = jnp.einsum('bhrnid,bhrnjd->bhrnij', qb, kb).astype(jnp.float32) * (hd ** -0.5)
    qi = jnp.arange(n_keys)[:, None]
    kj = jnp.arange(2 * n_keys)[None, :]
    dist = n_keys + qi - kj
    key_idx = (jnp.arange(n_blk)[:, None, None] - 1) * n_keys + kj
    valid = (dist >= 0) & (dist <= n_keys) & (key_idx >= 0)
    alibi = -slopes.astype(jnp.float32)[:, None, None, None, None] * (dist * dilation).astype(jnp.float32)
    scores = jnp.where(valid, scores + alibi, NEG_BIG)
    lse = jax.nn.logsumexp(scores, axis=-1)
    p = jnp.exp(scores - lse[..., None])
    o = jnp.einsum('bhrnij,bhrnjd->bhrnid', p.astype(v.dtype), vb)
    o = o.reshape(bsz, nh, dilation, n_blk * n_keys, hd)[:, :, :, :sub_len]
    o = o.transpose(0, 1, 3, 2, 4).reshape(bsz, nh, seq, hd)
    lse = lse.reshape(bsz, nh, dilation, n_blk * n_keys)[..., :sub_len]
    lse = lse.transpose(0, 1, 3, 2).reshape(bsz, nh, seq)
    return o, lse

def dilated_attention_mixer(h, w_in, q_norm_w, k_norm_w, w_out):
    bsz, seq, _ = h.shape
    proj = h @ w_in
    n_qkv = 3 * B_N_GROUPS * B_WIDTH
    qkv = proj[..., :n_qkv].reshape(bsz, seq, B_N_GROUPS, 3, B_HEADS, B_HEAD_DIM)
    g = proj[..., n_qkv:]
    n_total = B_N_GROUPS * B_HEADS
    slopes = jnp.exp2(-ALIBI_MAX_EXP * jnp.arange(1, n_total + 1, dtype=jnp.float32) / n_total)
    slopes = slopes.reshape(B_N_GROUPS, B_HEADS)
    outs, lses = [], []
    for gi, (window, dilation) in enumerate(DILATED_GROUPS):
        q = rms_norm(qkv[:, :, gi, 0], q_norm_w[gi]).transpose(0, 2, 1, 3)
        k = rms_norm(qkv[:, :, gi, 1], k_norm_w[gi]).transpose(0, 2, 1, 3)
        v = qkv[:, :, gi, 2].transpose(0, 2, 1, 3)
        o, lse = dilated_window_attention(q, k, v, window, dilation, slopes[gi])
        outs.append(o)
        lses.append(lse)
    weights = jax.nn.softmax(jnp.stack(lses), axis=0)
    o = jnp.einsum('gbhs,gbhsd->bshd', weights.astype(outs[0].dtype), jnp.stack(outs))
    o = o.reshape(bsz, seq, B_WIDTH)
    y = (o.astype(jnp.float32) * jax.nn.silu(g.astype(jnp.float32))).astype(h.dtype)
    return y @ w_out

def spatial_gating_mixer(h, w_in, v_norm_w, v_norm_b, w_s, b_s, w_out):
    bsz, seq, _ = h.shape
    u, v, g = jnp.split(h @ w_in, 3, axis=-1)
    u = jax.nn.gelu(u)
    v = layer_norm(jax.nn.gelu(v), v_norm_w, v_norm_b)
    v = v.reshape(bsz, seq // C_CHUNK, C_CHUNK, C_GROUPS, C_GROUP_DIM)
    w_causal = w_s * jnp.tril(jnp.ones((C_CHUNK, C_CHUNK), dtype=w_s.dtype))
    s = jnp.einsum('gts,bnsgc->bntgc', w_causal, v) + b_s.T[None, None, :, :, None]
    y = u * s.reshape(bsz, seq, C_WIDTH) * jax.nn.silu(g)
    return y @ w_out

def setup_inputs(seed: int = 0) -> dict:
    key = jax.random.key(seed)
    ks = jax.random.split(key, 16)
    nrm = jax.random.normal
    f32 = jnp.float32
    return {
        'x': nrm(ks[0], (BATCH, SEQ, D_MODEL), f32),
        'norm_w': 1.0 + 0.02 * nrm(ks[1], (DEPTH, D_MODEL), f32),
        'a_w_in': nrm(ks[2], (N_A_LAYERS, D_MODEL, 4 * A_WIDTH), f32) * D_MODEL ** -0.5,
        'a_lower_bounds': 0.1 * nrm(ks[3], (N_A_LAYERS, A_WIDTH), f32),
        'a_o_norm_w': 1.0 + 0.02 * nrm(ks[4], (N_A_LAYERS, A_HEAD_DIM), f32),
        'a_w_out': nrm(ks[5], (N_A_LAYERS, A_WIDTH, D_MODEL), f32) * A_WIDTH ** -0.5,
        'b_w_in': nrm(ks[6], (N_B_LAYERS, D_MODEL, (3 * B_N_GROUPS + 1) * B_WIDTH), f32) * D_MODEL ** -0.5,
        'b_q_norm_w': 1.0 + 0.02 * nrm(ks[7], (N_B_LAYERS, B_N_GROUPS, B_HEAD_DIM), f32),
        'b_k_norm_w': 1.0 + 0.02 * nrm(ks[8], (N_B_LAYERS, B_N_GROUPS, B_HEAD_DIM), f32),
        'b_w_out': nrm(ks[9], (N_B_LAYERS, B_WIDTH, D_MODEL), f32) * B_WIDTH ** -0.5,
        'c_w_in': nrm(ks[10], (N_C_LAYERS, D_MODEL, 3 * C_WIDTH), f32) * D_MODEL ** -0.5,
        'c_v_norm_w': 1.0 + 0.02 * nrm(ks[11], (N_C_LAYERS, C_WIDTH), f32),
        'c_v_norm_b': 0.02 * nrm(ks[12], (N_C_LAYERS, C_WIDTH), f32),
        'c_w_s': nrm(ks[13], (N_C_LAYERS, C_GROUPS, C_CHUNK, C_CHUNK), f32) * C_CHUNK ** -0.5,
        'c_b_s': 1.0 + 0.1 * nrm(ks[14], (N_C_LAYERS, C_GROUPS, C_CHUNK), f32),
        'c_w_out': nrm(ks[15], (N_C_LAYERS, C_WIDTH, D_MODEL), f32) * C_WIDTH ** -0.5,
    }

def reference(x, norm_w, a_w_in, a_lower_bounds, a_o_norm_w, a_w_out,
              b_w_in, b_q_norm_w, b_k_norm_w, b_w_out,
              c_w_in, c_v_norm_w, c_v_norm_b, c_w_s, c_b_s, c_w_out):
    lb_soft = jax.nn.softmax(a_lower_bounds.astype(jnp.float32), axis=0)
    lower_bounds = jnp.cumsum(lb_soft, axis=0) - lb_soft[0]
    for layer in range(DEPTH):
        h = rms_norm(x, norm_w[layer])
        kind, idx = layer % N_MIXERS, layer // N_MIXERS
        if kind == 0:
            y = hgrn2_mixer(h, a_w_in[idx], lower_bounds[idx], a_o_norm_w[idx], a_w_out[idx])
        elif kind == 1:
            y = dilated_attention_mixer(h, b_w_in[idx], b_q_norm_w[idx], b_k_norm_w[idx], b_w_out[idx])
        else:
            y = spatial_gating_mixer(h, c_w_in[idx], c_v_norm_w[idx], c_v_norm_b[idx],
                                     c_w_s[idx], c_b_s[idx], c_w_out[idx])
        x = x + y.astype(x.dtype)
    return x


_drawn_inputs = setup_inputs


def setup_inputs(seed=0):
    import zlib

    import numpy as np

    out = dict(_drawn_inputs(seed))
    spreads = {}
    factors = {'a_lower_bounds': 8.0,
     'a_o_norm_w': 3.845,
     'b_q_norm_w': 8.0,
     'b_k_norm_w': 8.0,
     'c_v_norm_w': 8.0,
     'c_v_norm_b': 8.0}
    for name, (base, spread) in spreads.items():
        noise = np.random.default_rng([zlib.crc32(name.encode()), seed]).standard_normal(out[name].shape)
        drawn = base * np.exp(spread * noise) if base else spread * noise
        out[name] = __import__('jax').numpy.asarray(drawn.astype(out[name].dtype))
    for name, factor in factors.items():
        out[name] = (out[name] * factor).astype(out[name].dtype)
    return out
```

```python
from contextlib import ExitStack

import numpy as np

import concourse.bass as bass
from concourse import mybir

F32 = mybir.dt.float32
F32R = mybir.dt.float32r
U8 = mybir.dt.uint8
ALU = mybir.AluOpType
ACT = mybir.ActivationFunctionType
AX = mybir.AxisListType.X

P = 128
D = 1024
S = 512
KT = D // P
TT = S // P
HEADS = D // P
EPS = 1e-6
LB_FLOOR = 1e-30

RAW = 4
HALF = 3
SLOTS = 2 * HALF + 1
A_PARTS = (1, 0, 2, 3)
B_PARTS = (0, 1, 2, 9, 3, 4, 5, 6, 7, 8)
A_CHUNKS, B_CHUNKS, OUT_CHUNKS = len(A_PARTS), len(B_PARTS), 8
C_V_CHUNKS, C_UG_CHUNKS = 8, 16
LEVELS = 7
G_STEPS = LEVELS + 3

SMALL_CONSTANTS = 8
GELU_SCALE = 2 * (2 / np.pi) ** 0.5
MASKED = -3e38
DIL = (1, 4, 16)
WINDOW = (128, 512, 2048)
B_UNITS = 12
B_STEPS = 8

LAYER_IN = (HEADS * A_CHUNKS, HEADS * B_CHUNKS, C_V_CHUNKS + C_UG_CHUNKS, HEADS * A_CHUNKS)
IN0 = [sum(LAYER_IN[:n]) + OUT_CHUNKS * n for n in range(4)]
OUT0 = [IN0[n] + LAYER_IN[n] for n in range(4)]

ACC_OF = (HEADS * A_CHUNKS, HEADS * (B_UNITS + 1), 4 * TT + C_UG_CHUNKS, HEADS * A_CHUNKS)
ACC0 = [sum(ACC_OF[:n]) for n in range(4)]


def a_ring(par, c):
    return c // 2 * HALF + c % 2


def b_half(par, g):
    return (par + g) % 2


def b_ring(par, c):
    if c == 3:
        return SLOTS - 1
    g, part = divmod(c if c < 3 else c - 1, 3)
    return b_half(par, g) * HALF + part


def b_unit(v):
    return v if v < 4 else v - 1


def pair_ring(c):
    return c // 2 % 2 * HALF + c % 2


def shape_constants():
    ident = np.eye(P, dtype=np.float32)
    a, q, r = np.meshgrid(np.arange(8), np.arange(4), np.arange(4), indexing="ij")
    perm = np.zeros((P, P), np.float32)
    perm[(16 * a + 4 * q + r).ravel(), (32 * r + 8 * q + a).ravel()] = 1
    s = np.arange(P)[:, None]
    masks = np.zeros((P, P * TT + LEVELS * 64 * TT), np.float32)
    masks[:, :P * TT] = np.tile(np.eye(P, dtype=np.float32), (1, TT))
    for n in range(LEVELS):
        m = 1 << n
        u = np.arange(64)
        t = (u // m) * 2 * m + m + u % m
        own = (s // (2 * m) == t // (2 * m)) & (s % (2 * m) < m)
        at = P * TT + n * 64 * TT
        masks[:, at:at + 64 * TT] = np.tile(own.astype(np.float32), (1, TT))
    p = np.arange(S)
    token = 16 * (p % 32) + 4 * (p // 32 % 4) + p // 128
    dist = token[:, None] - token[None, :]
    near = np.where((dist >= 0) & (dist <= WINDOW[0]), -dist, MASKED).astype(np.float32)
    own = dist[:P, :P]
    dil4 = np.where(own >= 0, -own, MASKED).astype(np.float32)
    dil16 = np.where((own >= 0) & (own % DIL[2] == 0), -own, MASKED).astype(np.float32)
    negdist = np.concatenate([near.reshape(TT, P, S).transpose(1, 0, 2).reshape(P, TT * S), dil4, dil16], 1)
    n = np.arange(1, 49, dtype=np.float32)
    slopes = np.tile(np.exp2(-8.0 * n / 48).astype(np.float32), (P, 1))
    causal = (np.arange(P)[:, None] >= np.arange(P)[None, :]).astype(np.float32)
    return {"c_ident": ident, "c_perm": perm, "c_masks": masks,
            "c_negdist": np.ascontiguousarray(negdist), "c_slopes": slopes, "c_causal": causal}


def build(nc, x, norm_w, a_w_in, a_lower_bounds, a_o_norm_w, a_w_out, b_w_in, b_q_norm_w, b_k_norm_w,
          b_w_out, c_w_in, c_v_norm_w, c_v_norm_b, c_w_s, c_b_s, c_w_out,
          c_ident, c_perm, c_masks, c_negdist, c_slopes, c_causal, out, layers=4):
    ctx = ExitStack()

    def sb(name, shape, dt=F32):
        return ctx.enter_context(nc.sbuf_tensor(name, shape, dt))

    def sem(name):
        return ctx.enter_context(nc.semaphore(name))

    with ctx:
        xt = sb("xt", [P, TT, D])
        op_hi = sb("op_hi", [P, KT, S], F32R)
        op_lo = sb("op_lo", [P, KT, S], F32R)
        y = sb("y", [P, KT, S])
        raw = sb("raw", [P, RAW, KT, P])
        w_hi = sb("w_hi", [P, SLOTS, KT, P], F32R)
        w_lo = sb("w_lo", [P, SLOTS, KT, P], F32R)
        xn = y[:, 0:4].rearrange("p (a b) c -> p a (b c)", a=2)
        norm_b = y[:, 4:6].rearrange("p b c -> p (b c)")
        ident = sb("ident", [P, P])
        perm = sb("perm", [P, P])
        stat = sb("stat", [P, 16])
        eps = sb("eps", [P, 1])
        vec_rows = sb("vec_rows", [24, P])
        vec = sb("vec", [P, 24])
        bound = sb("bound", [P, 5, 2, HEADS])
        scratch = sb("scratch", [P, 17008])

        def carve(start, *shape):
            n = int(np.prod(shape))
            assert start + n <= 17008
            v = scratch[:, start:start + n]
            if len(shape) == 2:
                v = v.rearrange("p (a b) -> p a b", a=shape[0])
            if len(shape) == 3:
                v = v.rearrange("p (a b c) -> p a b c", a=shape[0], b=shape[1])
            return v, start + n

        at = 0
        a_q, at = carve(at, 2, S)
        a_k, at = carve(at, 2, S)
        a_t, at = carve(at, 2, 2 * S)
        a_v, at = carve(at, 2, S)
        a_gate, at = carve(at, 2, S)
        a_sig, at = carve(at, 3, S)
        a_vt, at = carve(at, TT, P)
        a_sd, at = carve(at, TT, P)
        a_sx, at = carve(at, 6, P)
        a_sq, at = carve(at, TT, P)
        a_on, at = carve(at, TT, P)
        a_ss, at = carve(at, 3, TT)
        mask_f, at = carve(at, TT * P + LEVELS * TT * 64)
        a_mask = sb("a_mask", [P, TT * P + LEVELS * TT * 64], U8)
        at = 0
        b_raw, at = carve(at, B_UNITS, 256)
        b_qk, at = carve(at, 6, S)
        b_v, at = carve(at, 2, B_UNITS, P)
        b_gate, at = carve(at, 2, S)
        b_eg, at = carve(at, S)
        b_sq, at = carve(at, 256)
        b_s, at = carve(at, 2, 768)
        b_pt, at = carve(at, 2, 768)
        b_dist, at = carve(at, TT * S + 256)
        b_o, at = carve(at, TT, P)
        b_ss, at = carve(at, B_UNITS * 4)
        b_rs, at = carve(at, B_UNITS * 4)
        b_small, at = carve(at, 4, 2)
        slope = sb("slope", [P, 48])
        at = 0
        c_v, at = carve(at, TT, D)
        c_vw, at = carve(at, D)
        c_vb, at = carve(at, D)
        c_ws, at = carve(at, HEADS, P)
        c_wt, at = carve(at, HEADS, P)
        c_bs, at = carve(at, HEADS, P)
        c_x2, at = carve(at, 2, S)
        c_z, at = carve(at, 2, S)
        c_u, at = carve(at, 2, S)
        c_g, at = carve(at, 2, S)
        c_st, at = carve(at, TT, 12)
        c_mv, at = carve(at, TT, 4)
        causal, at = carve(at, P)
        ones = sb("ones", [1, P])

        ps = [ctx.enter_context(nc.psum_tensor(f"ps{n}", [P, S], F32)) for n in range(8)]
        acc = ps[0:2]
        score = ps[2:4]
        turn = ps[4:6]
        obank = ps[6]
        spare = ps[7]

        s_ident = sem("s_ident")
        s_const = sem("s_const")
        s_mask = sem("s_mask")
        s_dist = sem("s_dist")
        s_x = [sem(f"s_x{t}") for t in range(TT)]
        s_normw = sem("s_normw")
        raw_landed = [sem(f"raw_landed{n}") for n in range(RAW)]
        hi_done = sem("hi_done")
        lo_done = sem("lo_done")
        s_vecT = sem("s_vecT")
        s_bact = sem("s_bact")
        bound_step = sem("bound_step")
        vec_step = sem("vec_step")
        rstd_done = sem("rstd_done")
        sd_zero = sem("sd_zero")
        s_set = sem("s_set")
        ssq_done = sem("ssq_done")
        ms_done = sem("ms_done")
        root_done = sem("root_done")
        xn_done = sem("xn_done")
        xT_done = sem("xT_done")
        h_hi = sem("h_hi")
        h_lo = sem("h_lo")
        x_new = sem("x_new")
        out_ready = sem("out_ready")
        y_done = sem("y_done")
        y_hi = sem("y_hi")
        y_lo = sem("y_lo")
        acc_ready = sem("acc_ready")
        s_out = sem("s_out")
        f_act = sem("f_act")
        q_act = sem("q_act")
        v_act = sem("v_act")
        g_act = sem("g_act")
        kf_done = sem("kf_done")
        q_done = sem("q_done")
        gate_done = sem("gate_done")
        vT_ready = sem("vT_ready")
        vT_done = sem("vT_done")
        g_ready = sem("g_ready")
        sd_done = sem("sd_done")
        sx_done = sem("sx_done")
        upd = sem("upd")
        t_step = sem("t_step")
        rs_done = sem("rs_done")
        o_ready = sem("o_ready")
        sq_done = sem("sq_done")
        oms_done = sem("oms_done")
        oroot_done = sem("oroot_done")
        on_done = sem("on_done")
        oT_ready = sem("oT_ready")
        u_act = sem("u_act")
        u_dve = sem("u_dve")
        bms_done = sem("bms_done")
        broot_done = sem("broot_done")
        qn_done = sem("qn_done")
        qkT_ready = sem("qkT_ready")
        qkT_done = sem("qkT_done")
        s_ready = sem("s_ready")
        s_biased = sem("s_biased")
        m_done = sem("m_done")
        e_done = sem("e_done")
        pT_ready = sem("pT_ready")
        pT_act = sem("pT_act")
        pT_dve = sem("pT_dve")
        bo_ready = sem("bo_ready")
        bo_done = sem("bo_done")
        boT_ready = sem("boT_ready")
        eg_done = sem("eg_done")
        bg_step = sem("bg_step")
        brs_done = sem("brs_done")
        l_done = sem("l_done")
        bgate_done = sem("bgate_done")
        s_cvec = sem("s_cvec")
        cw_masked = sem("cw_masked")
        cwT_ready = sem("cwT_ready")
        cwT_done = sem("cwT_done")
        sqc_done = sem("sqc_done")
        z_done = sem("z_done")
        sig_done = sem("sig_done")
        gelu_done = sem("gelu_done")
        cms_done = sem("cms_done")
        croot_done = sem("croot_done")
        ln_done = sem("ln_done")
        sp_ready = sem("sp_ready")
        poly_done = sem("poly_done")
        cstat_done = sem("cstat_done")
        ln_step = sem("ln_step")
        cg_act = sem("cg_act")
        cgate_done = sem("cgate_done")
        cug_done = sem("cug_done")

        block = ctx.enter_context(nc.Block())

        def landed(n0, per, j, par, c):
            n = n0 + per * par + c
            return n % RAW, 16 * (n // RAW + 1) + 16 * (2 * per // RAW) * j

        def chunk(n0, per, j, par, c):
            return n0 + per * par + c + 2 * per * j

        def columns(w, col):
            return w[:, bass.ds(col, P)].rearrange("(k p) c -> p k c", p=P)

        def static(v):
            return isinstance(v, int)

        def iterations(eng, body, peeled=0):
            body(0, 0, True, False, False)
            body(0, 1, True, True, False)
            with eng.Fori(1, HEADS // 2 - peeled) as j:
                body(j, 0, True, True, True)
                body(j, 1, True, True, True)
            for j in range(HEADS // 2 - peeled, HEADS // 2):
                body(j, 0, True, True, True)
                body(j, 1, True, True, True)
            body(HEADS // 2, 0, False, True, True)
            body(HEADS // 2, 1, False, False, True)

        def terms(a, b):
            return ((a[0], b[0]), (a[1], b[0]), (a[0], b[1]))

        def h_part(buf, n, t, half):
            ks = slice(half * 4, half * 4 + 4)
            if n == 1:
                return buf[:, ks].rearrange("p k (r a) -> p k r a", a=32)[:, :, :, 8 * t:8 * t + 8]
            return buf[:, ks, t * P:(t + 1) * P]

        def turned_part(n, half):
            if n == 1:
                return turn[half][:].rearrange("p (k r a) -> p k r a", k=4, a=8)
            return turn[half][:].rearrange("p (k c) -> p k c", k=4)

        @block.sync
        def _(sp):
            def load(slot, src, n):
                if static(n):
                    if n >= RAW:
                        sp.wait_ge(lo_done, n - (RAW - 1))
                    sp.dma_start(raw[:, slot], src).then_inc(raw_landed[slot], 16)
                else:
                    split = sp.to_reg(n - (RAW - 1))
                    sp.dma_start(raw[:, slot], src).wait_op(lo_done, split, "sem-ge").then_inc(raw_landed[slot], 16)

            def load_columns(n0, w, cols):
                for c, col in enumerate(cols):
                    load((n0 + c) % RAW, columns(w, col), n0 + c)

            def load_layer(n, w, parts):
                per = len(parts)

                def body(j, par, proj, mix, end):
                    if proj:
                        for c, part in enumerate(parts):
                            col = j * (2 * P) + (part * D + par * P)
                            if not static(col):
                                col = sp.snap(col)
                            load(landed(IN0[n], per, j, par, c)[0], columns(w, col), chunk(IN0[n], per, j, par, c))
                iterations(sp, body)

            sp.dma_start(xt[:, 0], x[0, 0:P, :]).then_inc(s_x[0], 16)
            sp.dma_start(norm_b, norm_w[0:1, :].to_broadcast([P, D])).then_inc(s_normw, 16)
            for t in range(1, TT):
                sp.dma_start(xt[:, t], x[0, t * P:(t + 1) * P, :]).then_inc(s_x[t], 16)
            for n in range(layers):
                w_out = (a_w_out, b_w_out, c_w_out, a_w_out)[n][n // 3]
                if n:
                    sp.wait_ge(y_lo, KT * n)
                    sp.dma_start(norm_b, norm_w[n:n + 1, :].to_broadcast([P, D])).then_inc(s_normw, 16)
                if n % 3 == 0:
                    load_layer(n, a_w_in[n // 3], A_PARTS)
                if n == 1:
                    sp.wait_ge(y_done, KT)
                    sp.dma_start(b_dist, c_negdist).then_inc(s_dist, 16)
                    load_layer(n, b_w_in[0], B_PARTS)
                if n == 2:
                    sp.wait_ge(y_done, 2 * KT)
                    sp.dma_start(causal, c_causal).then_inc(s_cvec, 16)
                    sp.dma_start(c_ws, c_w_s[0].rearrange("g t s -> t g s")).then_inc(s_cvec, 16)
                    sp.dma_start(c_vw, c_v_norm_w[0:1, :].to_broadcast([P, D])).then_inc(s_cvec, 16)
                    sp.dma_start(c_vb, c_v_norm_b[0:1, :].to_broadcast([P, D])).then_inc(s_cvec, 16)
                    sp.dma_start(c_bs[0:1], c_b_s[0:1]).then_inc(s_cvec, 16)
                    load_columns(IN0[n], c_w_in[0], [D + c * P for c in range(C_V_CHUNKS)])
                    load_columns(IN0[n] + C_V_CHUNKS, c_w_in[0],
                                 [part * D + g * P for g in range(HEADS) for part in (0, 2)])
                load_columns(OUT0[n], w_out, [c * P for c in range(OUT_CHUNKS)])
            for t in range(TT):
                sp.wait_ge(x_new, (layers - 1) * 16 + 12 + t + 1)
                sp.dma_start(out[0, t * P:(t + 1) * P, :], xt[:, t]).then_inc(s_out, 16)
            sp.wait_ge(s_out, 16 * TT)

        @block.gpsimd
        def _(pool):
            pool.dma_start(ident[:], c_ident).then_inc(s_ident, 16)
            pool.dma_start(vec_rows[0:16, :], a_lower_bounds.rearrange("l (h p) -> (l h) p", p=P)).then_inc(s_const, 16)
            pool.dma_start(vec_rows[16:18, :], a_o_norm_w).then_inc(s_const, 16)
            for e in range(2):
                pool.dma_start(vec_rows[18:21, e * 64:(e + 1) * 64], b_q_norm_w[0]).then_inc(s_const, 16)
                pool.dma_start(vec_rows[21:24, e * 64:(e + 1) * 64], b_k_norm_w[0]).then_inc(s_const, 16)
            pool.dma_start(mask_f, c_masks).then_inc(s_mask, 16)
            pool.dma_start(perm[:], c_perm).then_inc(s_const, 16)
            pool.dma_start(slope[:], c_slopes).then_inc(s_const, 16)

            def split_lo(slot, ring, n):
                pool.wait_ge(hi_done, n + 1)
                nc.gpsimd.tensor_tensor(w_lo[:, ring], raw[:, slot], w_hi[:, ring].bitcast(F32),
                                        ALU.subtract).then_inc(lo_done, 1)

            def split_layer(n, per, rings):
                def body(j, par, proj, mix, end):
                    if proj:
                        for c in range(per):
                            split_lo(landed(IN0[n], per, j, par, c)[0], rings(par, c), chunk(IN0[n], per, j, par, c))
                iterations(pool, body)

            for n in range(layers):
                if n % 3 == 0:
                    split_layer(n, len(A_PARTS), a_ring)
                elif n == 1:
                    split_layer(n, len(B_PARTS), b_ring)
                else:
                    for c in range(LAYER_IN[n]):
                        split_lo((IN0[n] + c) % RAW, pair_ring(c), IN0[n] + c)
                for c in range(OUT_CHUNKS):
                    split_lo((OUT0[n] + c) % RAW, pair_ring(c), OUT0[n] + c)

        @block.tensor
        def _(pe):
            def feature_step(bank, ring, k):
                w = (w_hi[:, ring, k, :], w_lo[:, ring, k, :])
                h = (op_hi[:, k, :], op_lo[:, k, :])
                for p, (a, b) in enumerate(terms(w, h)):
                    last = nc.tensor.matmul(bank, a, b, start=(k == 0 and p == 0), stop=(k == KT - 1 and p == 2))
                return last

            def token_step(bank, ring, size, k, t):
                w = (w_hi[:, ring:ring + size, k, :], w_lo[:, ring:ring + size, k, :])
                h = (op_hi[:, k, t * P:(t + 1) * P], op_lo[:, k, t * P:(t + 1) * P])
                for p, (a, b) in enumerate(terms(h, w)):
                    last = nc.tensor.matmul(bank, a, b, start=(k == 0 and p == 0), stop=(k == KT - 1 and p == 2))
                return last

            def transpose_x(n):
                turned = perm if n == 1 else ident
                if n == 0:
                    pe.wait_ge(s_ident, 16)
                for t in range(TT):
                    pe.wait_ge(xn_done, TT * n + t + 1)
                    for half in range(2):
                        if t:
                            pe.wait_ge(h_lo, 8 * n + 2 * t - 1 + half)
                        for k in range(4):
                            kk = half * 4 + k
                            last = nc.tensor.transpose(turn[half][:, k * P:(k + 1) * P],
                                                       xn[:, t % 2, kk * P:(kk + 1) * P], turned[:])
                        last.then_inc(xT_done, 1)
                if n == 0:
                    pe.wait_ge(s_const, 16 * SMALL_CONSTANTS)
                    nc.tensor.transpose(spare[:, 0:24], vec_rows[:], ident[0:24, 0:24]).then_inc(s_vecT, 1)
                pe.wait_ge(h_lo, 8 * n + 8)

            def output_projection(n):
                pe.wait_ge(y_lo, KT * (n + 1))
                for b in range(4):
                    pe.wait_ge(lo_done, OUT0[n] + 2 * b + 2)
                    for t in range(TT):
                        u = 4 * b + t
                        if u >= 2:
                            pe.wait_ge(x_new, 16 * n + u - 1)
                        for k in range(KT):
                            last = token_step(acc[u % 2][:, 0:256], pair_ring(2 * b), 2, k, t)
                        last.then_inc(out_ready, 1)

            def layer_a(n, idx):
                H0 = HEADS * idx

                def body(j, par, proj, mix, end):
                    i = j * 2 + par
                    h = i + (H0 - 1)
                    prev = 1 - par
                    later = not static(h) or h > H0

                    def turn_v():
                        pe.wait_ge(v_act, h + 1)
                        if later:
                            pe.wait_ge(vT_done, h)
                        for t in range(TT):
                            last = nc.tensor.transpose(turn[0][:, t * P:(t + 1) * P],
                                                       a_v[:, prev, t * P:(t + 1) * P], ident[:])
                        last.then_inc(vT_ready, 1)

                    def scores(g):
                        q, k, bank = a_q[:, prev], a_k[:, prev], score[g % 2]
                        if g == 0:
                            pe.wait_ge(q_done, h + 1)
                        else:
                            pe.wait_ge(upd, h * 9 + g)
                        if g >= 2:
                            pe.wait_ge(sd_done, h * 8 + (g - 1))
                        elif later:
                            pe.wait_ge(sx_done, h * 2 + (g - 1))
                        if g == 0:
                            for t in range(TT):
                                tile = slice(t * P, (t + 1) * P)
                                last = nc.tensor.matmul(bank[:, tile], k[:, tile], q[:, tile], start=True, stop=True)
                        elif g <= LEVELS:
                            m = 1 << (g - 1)
                            upper = q.rearrange("p (t b u m) -> p t b u m", t=TT, u=2, m=m)
                            for t in range(TT):
                                last = nc.tensor.matmul(bank[:, t * 64:(t + 1) * 64], k[:, t * P:(t + 1) * P],
                                                        upper[:, t, :, 1, :], start=True, stop=True)
                        elif g == LEVELS + 1:
                            for s in (0, 2):
                                last = nc.tensor.matmul(bank[:, s * 64:s * 64 + P], k[:, s * P:(s + 1) * P],
                                                        q[:, (s + 1) * P:(s + 2) * P], start=True, stop=True)
                        else:
                            for s in (0, 1):
                                last = nc.tensor.matmul(bank[:, s * 256:(s + 1) * 256], k[:, s * P:(s + 1) * P],
                                                        q[:, 2 * P:4 * P], start=True, stop=True)
                        last.then_inc(g_ready, 1)

                    def values():
                        pe.wait_ge(sd_done, h * 8 + 8)
                        pe.wait_ge(sx_done, h * 2 + 2)
                        pe.wait_ge(vT_done, h + 1)
                        if later:
                            pe.wait_ge(on_done, h)
                        pairs = (((a_sd[:, 0], 0),),
                                 ((a_sd[:, 1], 1), (a_sx[:, 0], 0)),
                                 ((a_sd[:, 2], 2), (a_sx[:, 2], 0), (a_sx[:, 4], 1)),
                                 ((a_sd[:, 3], 3), (a_sx[:, 1], 2), (a_sx[:, 3], 0), (a_sx[:, 5], 1)))
                        for t in range(TT):
                            for c, (weights, s) in enumerate(pairs[t]):
                                last = nc.tensor.matmul(obank[:, t * P:(t + 1) * P], weights, a_vt[:, s],
                                                        start=(c == 0), stop=(c == len(pairs[t]) - 1))
                        last.then_inc(o_ready, 1)

                    def turn_o():
                        pe.wait_ge(on_done, h)
                        if not static(i) or i > 2:
                            pe.wait_ge(y_done, i + (KT * n - 2))
                        for t in range(TT):
                            last = nc.tensor.transpose(turn[1][:, t * P:(t + 1) * P], a_on[:, t], ident[:])
                        last.then_inc(oT_ready, 1)

                    def bank_free(c):
                        first = static(i) and i == 0
                        if c == 0 and not first:
                            pe.wait_ge(v_act, i + H0)
                        if c == 1 and not first:
                            pe.wait_ge(gate_done, i + H0)
                        if c == 2:
                            pe.wait_ge(f_act, i + (H0 + 1))
                        if c == 3:
                            pe.wait_ge(q_done, i + (H0 + 1))

                    steps = {}
                    if mix:
                        steps[1] = [turn_v]
                        for g in range(G_STEPS):
                            steps.setdefault(int(2 + 2.4 * g), []).append(lambda g=g: scores(g))
                        steps[27] = [values]
                    if end:
                        steps.setdefault(3, []).append(turn_o)
                    for ks in range(len(A_PARTS) * KT):
                        c, k = divmod(ks, KT)
                        if proj:
                            if k == 0:
                                pe.wait_ge(lo_done, chunk(IN0[n], len(A_PARTS), j, par, c) + 1)
                                bank_free(c)
                            last = feature_step(acc[c % 2][:], a_ring(par, c), k)
                            if k == KT - 1:
                                last.then_inc(acc_ready, 1)
                        for step in steps.get(ks, ()):
                            step()

                iterations(pe, body)

            def layer_b(n):
                def body(j, par, proj, mix, end):
                    i = j * 2 + par
                    h = i - 1
                    prev = 1 - par
                    later = not static(h) or h > 0

                    def turn_qk(b):
                        g, part = divmod(b, 2)
                        pe.wait_ge(qn_done, h * 3 + (g + 1))
                        if b >= 2:
                            pe.wait_ge(qkT_done, h * 6 + (b - 1))
                        elif later:
                            pe.wait_ge(y_done, h + KT * n)
                        for t in range(TT):
                            last = nc.tensor.transpose(turn[b % 2][:, t * P:(t + 1) * P],
                                                       b_raw[:, g * 4 + t, part * P:(part + 1) * P], ident[:])
                        last.then_inc(qkT_ready, 1)

                    def scores(a):
                        e, t = divmod(a, TT)
                        head, tile = slice(e * 64, e * 64 + 64), slice(t * P, (t + 1) * P)
                        if a == 0:
                            pe.wait_ge(qkT_done, h * 6 + 6)
                        if a or later:
                            pe.wait_ge(s_biased, h * 8 + a)
                        nc.tensor.matmul(score[0][:], b_qk[head, 0, tile], b_qk[head, 1, :], start=True, stop=True)
                        nc.tensor.matmul(score[1][:, 0:P], b_qk[head, 2, tile], b_qk[head, 3, tile], start=True, stop=True)
                        nc.tensor.matmul(score[1][:, P:2 * P], b_qk[head, 4, tile], b_qk[head, 5, tile],
                                         start=True, stop=True).then_inc(s_ready, 1)

                    def turn_p(a):
                        pe.wait_ge(e_done, h * 8 + (a + 1))
                        if a:
                            pe.wait_ge(pT_act, h * 8 + a)
                            pe.wait_ge(pT_dve, h * 8 + a)
                        for c in range(6):
                            last = nc.tensor.transpose(turn[c // 4][:, c % 4 * P:(c % 4 + 1) * P],
                                                       b_s[:, a % 2, c * P:(c + 1) * P], ident[:])
                        last.then_inc(pT_ready, 1)

                    def values(a):
                        e, t = divmod(a, TT)
                        pe.wait_ge(pT_act, h * 8 + (a + 1))
                        pe.wait_ge(pT_dve, h * 8 + (a + 1))
                        if a >= 2 or later:
                            pe.wait_ge(bo_done, h * 8 + (a - 1))
                        for c in range(6):
                            unit = c if c < 4 else (c - 3) * TT + t
                            last = nc.tensor.matmul((obank, spare)[a % 2][:, 0:64], b_pt[:, a % 2, c * P:(c + 1) * P],
                                                    b_v[:, prev, unit, e * 64:(e + 1) * 64],
                                                    start=(c == 0), stop=(c == 5))
                        last.then_inc(bo_ready, 1)

                    def turn_o():
                        pe.wait_ge(bo_done, h * 8 + 8)
                        for t in range(TT):
                            last = nc.tensor.transpose(turn[0][:, t * P:(t + 1) * P], b_o[:, t], ident[:])
                        last.then_inc(boT_ready, 1)

                    def bank_free(v):
                        if v in (0, 1) and not (static(i) and i == 0):
                            pe.wait_ge(u_act, i * 12 + (v - 1))
                            pe.wait_ge(u_dve, i * 12 + (v - 1))
                        elif v == 6:
                            pe.wait_ge(bgate_done, i + 1)
                        elif v >= 2:
                            u = b_unit(v - 2)
                            pe.wait_ge(u_act, i * 12 + (u + 1))
                            pe.wait_ge(u_dve, i * 12 + (u + 1))

                    steps = {}
                    if mix:
                        for b in range(6):
                            steps[2 + 2 * b] = [lambda b=b: turn_qk(b)]
                        for s in range(B_STEPS + 2):
                            at = steps.setdefault(16 + 9 * s, [])
                            if s < B_STEPS:
                                at.append(lambda a=s: scores(a))
                            if 1 <= s <= B_STEPS:
                                at.append(lambda a=s - 1: turn_p(a))
                            if s >= 2:
                                at.append(lambda a=s - 2: values(a))
                        steps[101] = [turn_o]
                    for ks in range((B_UNITS + 1) * KT):
                        v, k = divmod(ks, KT)
                        if proj:
                            bank = acc[(par + v) % 2]
                            if k == 0:
                                if v in (0, 4, 5, 9):
                                    upto = {0: 3, 4: 4, 5: 7, 9: 10}[v]
                                    pe.wait_ge(lo_done, chunk(IN0[n], len(B_PARTS), j, par, upto))
                                bank_free(v)
                            if v == 4:
                                last = feature_step(bank[:], SLOTS - 1, k)
                            else:
                                g, t = divmod(b_unit(v), TT)
                                last = token_step(bank[:, 0:3 * P], b_half(par, g) * HALF, 3, k, t)
                            if k == KT - 1:
                                last.then_inc(acc_ready, 1)
                        for step in steps.get(ks, ()):
                            step()

                iterations(pe, body)

            def layer_c(n):
                pe.wait_ge(cw_masked, 1)
                for g in range(HEADS):
                    last = nc.tensor.transpose(turn[g // 4][:, g % 4 * P:(g % 4 + 1) * P], c_ws[:, g], ident[:])
                last.then_inc(cwT_ready, 1)

                def spatial(g):
                    pe.wait_ge(ln_done, TT)
                    pe.wait_ge(cwT_done, 1)
                    if g >= 2:
                        pe.wait_ge(y_done, KT * n + g - 1)
                    for t in range(TT):
                        tile = score[g % 2][:, t * P:(t + 1) * P]
                        nc.tensor.matmul(tile, c_v[:, t, g * P:(g + 1) * P], c_wt[:, g], start=True, stop=False)
                        last = nc.tensor.matmul(tile, ones[0:1, :], c_bs[0:1, g], start=False, stop=True)
                    last.then_inc(sp_ready, 1)

                for p in range(LAYER_IN[n] // 2):
                    if p < 4:
                        pe.wait_ge(lo_done, IN0[n] + 2 * p + 2)
                        for t in range(TT):
                            u = 4 * p + t
                            if u >= 2:
                                pe.wait_ge(gelu_done, u - 1)
                            for k in range(KT):
                                last = token_step(acc[u % 2][:, 0:256], pair_ring(2 * p), 2, k, t)
                            last.then_inc(acc_ready, 1)
                        continue
                    for c in range(2):
                        pe.wait_ge(lo_done, IN0[n] + 2 * p + c + 1)
                        if c == 0:
                            pe.wait_ge(gelu_done, 15 if p == 4 else 12 + p)
                        if c == 1 and p > 4:
                            pe.wait_ge(cgate_done, p - 4)
                        if c == 1 and p == 4:
                            pe.wait_ge(gelu_done, 16)
                        for k in range(KT):
                            last = feature_step(acc[c][:], pair_ring(2 * p + c), k)
                        last.then_inc(acc_ready, 1)
                    if p >= 7:
                        spatial(p - 7)
                for g in range(5, HEADS):
                    spatial(g)

            for n in range(layers):
                transpose_x(n)
                if n % 3 == 0:
                    layer_a(n, n // 3)
                elif n == 1:
                    layer_b(n)
                else:
                    layer_c(n)
                output_projection(n)

        @block.scalar
        def _(act):
            def split_hi(slot, landed_at, ring, n):
                act.wait_ge(raw_landed[slot], landed_at)
                nc.scalar.activation(w_hi[:, ring], raw[:, slot], ACT.Copy).then_inc(hi_done, 1)

            def split_chunks(n0, per, j, par, chunks, ring):
                for c in chunks:
                    slot, at = landed(n0, per, j, par, c)
                    split_hi(slot, at, ring(par, c), None)

            def split_pair(n0, p):
                for c in (2 * p, 2 * p + 1):
                    split_hi((n0 + c) % RAW, 16 * ((n0 + c) // RAW + 1), pair_ring(c), None)

            def split_first(n):
                if n >= layers:
                    return
                if n:
                    act.wait_ge(out_ready, 16 * (n - 1) + 12)
                if n % 3 == 0:
                    split_chunks(IN0[n], len(A_PARTS), 0, 0, (0, 1), a_ring)
                elif n == 1:
                    split_chunks(IN0[n], len(B_PARTS), 0, 0, (0, 1, 2), b_ring)
                else:
                    split_pair(IN0[n], 0)

            def norm(n):
                for t in range(TT):
                    if n == 0:
                        act.wait_ge(s_x[t], 16)
                    else:
                        act.wait_ge(x_new, 16 * (n - 1) + 12 + t + 1)
                    if t == 0 and n == 0:
                        act.wait_ge(s_set, 1)
                    if TT * n + t >= 2:
                        act.wait_ge(xT_done, 8 * n + 2 * t - 2)
                    nc.scalar.activation(xn[:, t % 2], xt[:, t], ACT.Square,
                                         accum_out=stat[:, t:t + 1]).then_inc(ssq_done, 1)
                    act.wait_ge(ssq_done, TT * n + t + 1)
                    nc.scalar.activation(stat[:, 4 + t:5 + t], stat[:, t:t + 1], ACT.Sqrt, scale=1.0 / D,
                                         bias=eps[:]).then_inc(root_done, 1)
                    if n == 0 and t == 2:
                        split_first(0)
                    if t:
                        h_hi_parts(n, t - 1)
                h_hi_parts(n, TT - 1)

            def h_hi_parts(n, t):
                if n == 1 and t == 0:
                    act.wait_ge(out_ready, 16)
                for half in range(2):
                    act.wait_ge(xT_done, 8 * n + 2 * t + half + 1)
                    nc.scalar.activation(h_part(op_hi, n, t, half), turned_part(n, half),
                                         ACT.Copy).then_inc(h_hi, 1)

            def split_y(n, k):
                act.wait_ge(y_done, KT * n + k + 1)
                nc.scalar.activation(op_hi[:, k], y[:, k], ACT.Copy).then_inc(y_hi, 1)

            def output_chunks(n):
                for p in range(1, 4):
                    if p == 1:
                        act.wait_ge(acc_ready, ACC0[n] + ACC_OF[n])
                    else:
                        act.wait_ge(out_ready, 16 * n + 4 * p - 4)
                    split_pair(OUT0[n], p)
                split_first(n + 1)

            def layer_a(n, idx):
                H0, A0, per = HEADS * idx, ACC0[n], len(A_PARTS)

                def body(j, par, proj, mix, end):
                    i = j * 2 + par
                    h = i + (H0 - 1)
                    later = not static(h) or h > H0

                    if mix:
                        act.wait_ge(acc_ready, i * 4 + A0)
                        if not static(h) or h > 0:
                            act.wait_ge(gate_done, h)
                        nc.scalar.activation(a_sig[:, 1], acc[1][:], ACT.Sigmoid).then_inc(g_act, 1)
                        act.wait_ge(vT_ready, h + 1)
                        if later:
                            act.wait_ge(o_ready, h)
                        nc.scalar.activation(a_vt, turn[0][:].rearrange("p (t c) -> p t c", t=TT),
                                             ACT.Copy).then_inc(vT_done, 1)
                    if proj:
                        if static(i) and i == 0:
                            if n:
                                act.wait_ge(out_ready, 16 * n)
                        else:
                            act.wait_ge(acc_ready, i * 4 + A0)
                        split_chunks(IN0[n], per, j, par, (2, 3), a_ring)
                        act.wait_ge(acc_ready, i * 4 + (A0 + 1))
                        if not (static(i) and i < 2):
                            act.wait_ge(g_ready, i * G_STEPS + G_STEPS * (H0 - 1))
                        if not (static(i) and i + H0 == 0):
                            act.wait_ge(kf_done, i + H0)
                        nc.scalar.activation(a_t[:, par, 0:S], acc[0][:], ACT.Sigmoid)
                        nc.scalar.activation(a_sig[:, 2], acc[0][:], ACT.Sigmoid, scale=-1.0).then_inc(f_act, 1)
                        act.wait_ge(acc_ready, i * 4 + (A0 + 2))
                        if not (static(i) and i + H0 == 0):
                            act.wait_ge(q_done, i + H0)
                        nc.scalar.activation(a_sig[:, 0], acc[1][:], ACT.Sigmoid).then_inc(q_act, 1)
                        split_chunks(IN0[n], per, j if par == 0 else j + 1, 1 - par, (0, 1), a_ring)
                    if mix:
                        act.wait_ge(g_ready, h * G_STEPS + (LEVELS + 2))
                        if later:
                            act.wait_ge(o_ready, h)
                        nc.scalar.activation(a_sx[:, 0:2], score[0][:, 0:256].rearrange("p (t c) -> p t c", t=2),
                                             ACT.Copy).then_inc(sx_done, 1)
                        act.wait_ge(g_ready, h * G_STEPS + (LEVELS + 3))
                        nc.scalar.activation(a_sx[:, 2:6], score[1][:].rearrange("p (t c) -> p t c", t=4),
                                             ACT.Copy).then_inc(sx_done, 1)
                    if proj:
                        act.wait_ge(acc_ready, i * 4 + (A0 + 3))
                        if not (static(i) and i < 2):
                            act.wait_ge(vT_ready, i + (H0 - 1))
                        nc.scalar.activation(a_v[:, par], acc[0][:], ACT.Copy).then_inc(v_act, 1)
                    if mix:
                        act.wait_ge(o_ready, h + 1)
                        if not static(h) or h > 0:
                            act.wait_ge(oms_done, h)
                        nc.scalar.activation(a_sq, obank[:].rearrange("p (t c) -> p t c", t=TT),
                                             ACT.Square).then_inc(sq_done, 1)
                        act.wait_ge(oms_done, h + 1)
                        if not static(h) or h > 0:
                            act.wait_ge(rs_done, h)
                        nc.scalar.activation(a_ss[:, 1], a_ss[:, 0], ACT.Sqrt, scale=1.0 / P,
                                             bias=eps[:]).then_inc(oroot_done, 1)

                iterations(act, body)

            def layer_b(n):
                B0, per = ACC0[n], len(B_PARTS)

                def body(j, par, proj, mix, end):
                    i = j * 2 + par
                    h = i - 1
                    later = not static(h) or h > 0
                    prev = 1 - par

                    def qk_out(b):
                        act.wait_ge(qkT_ready, h * 6 + (b + 1))
                        if later:
                            act.wait_ge(s_ready, h * 8)
                        g, part = divmod(b, 2)
                        col = 18 + 3 * part + g
                        nc.scalar.activation(b_qk[:, b], turn[b % 2][:], ACT.Copy,
                                             scale=vec[:, col:col + 1]).then_inc(qkT_done, 1)

                    def exps(a):
                        act.wait_ge(m_done, h * 8 + (a + 1))
                        if a >= 2 or later:
                            act.wait_ge(l_done, h * 8 + (a - 1))
                        nc.scalar.activation(b_s[:, a % 2], b_s[:, a % 2], ACT.Exp, bias=b_small[:, 0, a % 2:a % 2 + 1],
                                             accum_out=b_small[:, 1, a % 2:a % 2 + 1]).then_inc(e_done, 1)

                    def p_out(a):
                        act.wait_ge(pT_ready, h * 8 + (a + 1))
                        if a >= 2 or later:
                            act.wait_ge(bo_ready, h * 8 + (a - 1))
                        nc.scalar.activation(b_pt[:, a % 2, 0:S], turn[0][:], ACT.Copy).then_inc(pT_act, 1)

                    def unit(v):
                        u = b_unit(v)
                        bank = acc[(par + v) % 2]
                        act.wait_ge(acc_ready, i * 13 + (B0 + v + 1))
                        if not (static(i) and i == 0 and u == 0):
                            act.wait_ge(u_dve, i * 12 + u)
                        nc.scalar.activation(b_sq, bank[:, 0:256], ACT.Square)
                        if u == 0 and not (static(i) and i < 2):
                            act.wait_ge(bo_ready, i * 8 - 8)
                        nc.scalar.activation(b_v[:, par, u], bank[:, 256:384], ACT.Copy).then_inc(u_act, 1)

                    def gate():
                        act.wait_ge(acc_ready, i * 13 + (B0 + 5))
                        if not (static(i) and i == 0):
                            act.wait_ge(bgate_done, i)
                        nc.scalar.activation(b_eg, acc[par][:], ACT.Exp, scale=-1.0).then_inc(eg_done, 1)

                    def roots():
                        act.wait_ge(u_dve, i * 12 + 12)
                        if not (static(i) and i == 0):
                            act.wait_ge(qn_done, i * 3)
                        nc.scalar.activation(b_rs, b_ss, ACT.Sqrt, scale=1.0 / 64, bias=eps[:]).then_inc(broot_done, 1)

                    def chunks(cs, sem_, value):
                        if value is not None:
                            act.wait_ge(sem_, value)
                        split_chunks(IN0[n], per, j, par, cs, b_ring)

                    def next_group0():
                        act.wait_ge(acc_ready, i * 13 + (B0 + 9))
                        if static(i) and i == HEADS - 1:
                            split_pair(OUT0[n], 0)
                        else:
                            split_chunks(IN0[n], per, j if par == 0 else j + 1, 1 - par, (0, 1, 2), b_ring)

                    plan = []
                    if proj:
                        first = static(i) and i == 0
                        plan.append((1, lambda: chunks((3,), acc_ready, None if first else i * 13 + B0)))
                        if first:
                            plan.append((1.1, lambda: chunks((4, 5, 6), out_ready, 16)))
                        else:
                            plan.append((1.1, lambda: chunks((4, 5, 6), acc_ready, i * 13 + B0)))
                        plan.append((33, lambda: chunks((7, 8, 9), acc_ready, i * 13 + (B0 + 4))))
                        plan.append((73, next_group0))
                        for v in range(B_UNITS + 1):
                            plan.append((8 * v + 8, gate if v == 4 else lambda v=v: unit(v)))
                        plan.append((104.5, roots))
                    if mix:
                        for b in range(6):
                            plan.append((3 + 2 * b, lambda b=b: qk_out(b)))
                        for a in range(B_STEPS):
                            plan.append((16 + 9 * a + 4, lambda a=a: exps(a)))
                            plan.append((16 + 9 * a + 10.5, lambda a=a: p_out(a)))
                    for _, step in sorted(plan, key=lambda p: p[0]):
                        step()

                iterations(act, body, peeled=1)

            def layer_c(n):
                C0 = ACC0[n]
                act.wait_ge(cwT_ready, 1)
                for half in range(2):
                    last = nc.scalar.activation(c_wt[:, half * 4:half * 4 + 4],
                                                turn[half][:].rearrange("p (g c) -> p g c", g=4), ACT.Copy)
                last.then_inc(cwT_done, 1)

                def gelu(u, bank, width):
                    if u >= 2:
                        act.wait_ge(z_done, u - 1)
                    nc.scalar.activation(c_x2[:, u % 2, 0:width], bank, ACT.Square).then_inc(sqc_done, 1)
                    act.wait_ge(z_done, u + 1)
                    nc.scalar.activation(c_z[:, u % 2, 0:width], c_z[:, u % 2, 0:width], ACT.Sigmoid,
                                         scale=GELU_SCALE).then_inc(sig_done, 1)

                for p in range(LAYER_IN[n] // 2):
                    def next_pair():
                        before = C0 + (4 * p if p <= 4 else 16 + 2 * (p - 4))
                        if p == 0:
                            act.wait_ge(out_ready, 16 * n)
                        else:
                            act.wait_ge(acc_ready, before)
                        if p + 1 < LAYER_IN[n] // 2:
                            split_pair(IN0[n], p + 1)
                        else:
                            split_pair(OUT0[n], 0)
                    next_pair()
                    if p < 4:
                        for t in range(TT):
                            u = 4 * p + t
                            act.wait_ge(acc_ready, C0 + u + 1)
                            gelu(u, acc[u % 2][:, 0:256], 256)
                        if p == 3:
                            for t in range(TT):
                                act.wait_ge(cms_done, t + 1)
                                nc.scalar.activation(c_mv[:, t, 2:3], c_mv[:, t, 1:2], ACT.Sqrt,
                                                     bias=eps[:]).then_inc(croot_done, 1)
                        continue
                    g = p - 4
                    act.wait_ge(acc_ready, C0 + 16 + 2 * g + 1)
                    gelu(16 + g, acc[0][:], S)
                    act.wait_ge(acc_ready, C0 + 16 + 2 * g + 2)
                    if g >= 1:
                        act.wait_ge(cgate_done, g)
                    nc.scalar.activation(c_g[:, 0], acc[1][:], ACT.Sigmoid).then_inc(cg_act, 1)

            norm(0)
            act.wait_ge(bound_step, 1)
            nc.scalar.activation(bound[:, 2], bound[:, 2], ACT.Exp).then_inc(s_bact, 1)
            for n in range(layers):
                if n:
                    norm(n)
                if n % 3 == 0:
                    layer_a(n, n // 3)
                elif n == 1:
                    layer_b(n)
                else:
                    layer_c(n)
                for k in range(KT):
                    if k == 0:
                        act.wait_ge(acc_ready, ACC0[n] + ACC_OF[n])
                    split_y(n, k)
                output_chunks(n)

        @block.vector
        def _(dve):
            def norm(n):
                for t in range(TT):
                    dve.wait_ge(root_done, TT * n + t + 1)
                    nc.vector.reciprocal(stat[:, 8 + t:9 + t], stat[:, 4 + t:5 + t]).then_inc(rstd_done, 1)
                    dve.wait_ge(rstd_done, TT * n + t + 1)
                    if t == 0:
                        dve.wait_ge(s_normw, 16 * (n + 1))
                    nc.vector.scalar_tensor_tensor(xn[:, t % 2], xt[:, t], stat[:, 8 + t:9 + t], norm_b,
                                                   ALU.mult, ALU.mult).then_inc(xn_done, 1)
                    if t:
                        h_lo_parts(n, t - 1)
                h_lo_parts(n, TT - 1)

            def h_lo_parts(n, t):
                for half in range(2):
                    dve.wait_ge(h_hi, 8 * n + 2 * t + half + 1)
                    nc.vector.tensor_tensor(h_part(op_lo, n, t, half), turned_part(n, half),
                                            h_part(op_hi, n, t, half).bitcast(F32), ALU.subtract).then_inc(h_lo, 1)

            def split_y(n, k):
                dve.wait_ge(y_hi, KT * n + k + 1)
                nc.vector.tensor_tensor(op_lo[:, k], y[:, k], op_hi[:, k].bitcast(F32),
                                        ALU.subtract).then_inc(y_lo, 1)

            def residual(n):
                for b in range(4):
                    cols = slice(b * 256, (b + 1) * 256)
                    for t in range(TT):
                        u = 4 * b + t
                        dve.wait_ge(out_ready, 16 * n + u + 1)
                        nc.vector.tensor_tensor(xt[:, t, cols], xt[:, t, cols], acc[u % 2][:, 0:256],
                                                ALU.add).then_inc(x_new, 1)

            def bounds():
                steps = [0]

                def step(ins):
                    steps[0] += 1
                    ins.then_inc(bound_step, 1)
                    dve.wait_ge(bound_step, steps[0])

                dve.wait_ge(s_vecT, 1)
                nc.vector.tensor_copy(vec[:], spare[:, 0:24]).then_inc(vec_step, 1)
                dve.wait_ge(vec_step, 1)
                l0, l1 = vec[:, 0:8], vec[:, 8:16]
                b = [bound[:, c, l] for c in range(5) for l in range(2)]
                nc.vector.tensor_scalar(vec[:, 18:21], vec[:, 18:21], 64 ** -0.5, None, ALU.mult)
                nc.vector.tensor_tensor(b[8], l0, l1, ALU.max).then_inc(vec_step, 1)
                dve.wait_ge(vec_step, 2)
                nc.vector.tensor_tensor(b[4], l0, b[8], ALU.subtract)
                step(nc.vector.tensor_tensor(b[5], l1, b[8], ALU.subtract))
                dve.wait_ge(s_bact, 1)
                step(nc.vector.tensor_tensor(b[8], b[4], b[5], ALU.add))
                step(nc.vector.reciprocal(b[9], b[8]))
                nc.vector.tensor_tensor(b[6], b[4], b[9], ALU.mult)
                step(nc.vector.tensor_tensor(b[7], b[5], b[9], ALU.mult))
                step(nc.vector.tensor_tensor(b[5], b[6], b[7], ALU.add))
                nc.vector.tensor_tensor(b[4], b[6], b[6], ALU.subtract)
                step(nc.vector.tensor_tensor(b[5], b[5], b[6], ALU.subtract))
                nc.vector.tensor_scalar(bound[:, 0], bound[:, 2], LB_FLOOR, None, ALU.max)
                step(nc.vector.tensor_scalar(bound[:, 1], bound[:, 2], -1.0, 1.0, ALU.mult, ALU.add))

            def layer_a(n, idx):
                H0 = HEADS * idx
                if n == 0:
                    dve.wait_ge(s_mask, 16)
                    nc.vector.tensor_copy(a_mask[:], mask_f)
                nc.vector.memset(a_sd, 0.0).then_inc(sd_zero, 1)
                dve.wait_ge(sd_zero, idx + 1)

                def body(j, par, proj, mix, end):
                    i = j * 2 + par
                    h = i + (H0 - 1)
                    prev = 1 - par
                    later = not static(h) or h > H0

                    def gate():
                        dve.wait_ge(g_act, h + 1)
                        nc.vector.tensor_tensor(a_gate[:, prev], acc[1][:], a_sig[:, 1], ALU.mult).then_inc(gate_done, 1)

                    def forget():
                        dve.wait_ge(f_act, i + (H0 + 1))
                        one_minus, floor = bound[:, 1, idx, bass.ds(i, 1)], bound[:, 0, idx, bass.ds(i, 1)]
                        nc.vector.tensor_scalar(a_t[:, par, 0:S], a_t[:, par, 0:S], one_minus, floor, ALU.mult, ALU.add)
                        nc.vector.tensor_scalar(a_k[:, par], a_sig[:, 2], one_minus, None, ALU.mult).then_inc(kf_done, 1)
                        dve.wait_ge(kf_done, i + (H0 + 1))

                    def decays(which):
                        for s in which:
                            size = S >> s
                            at = 2 * S - 2 * size
                            pairs = a_t[:, par, at:at + size].rearrange("p (b u) -> p b u", u=2)
                            nc.vector.tensor_tensor(a_t[:, par, at + size:at + size + size // 2],
                                                    pairs[:, :, 0], pairs[:, :, 1], ALU.mult).then_inc(t_step, 1)
                            dve.wait_ge(t_step, i * LEVELS + (LEVELS * H0 + s + 1))

                    def query():
                        dve.wait_ge(q_act, i + (H0 + 1))
                        nc.vector.tensor_tensor(a_q[:, par], acc[1][:], a_sig[:, 0], ALU.mult).then_inc(q_done, 1)

                    def move_on(g):
                        dve.wait_ge(g_ready, h * G_STEPS + (g + 1))
                        if 0 < g < 8:
                            dve.wait_ge(sd_done, h * 8 + g)
                        elif g == 0 and later:
                            dve.wait_ge(o_ready, h)
                        if g == 0:
                            nc.vector.tensor_tensor(a_q[:, prev], a_q[:, prev], a_t[:, prev, 0:S],
                                                    ALU.mult).then_inc(upd, 1)
                            return
                        m = 1 << (g - 1)
                        nb = S // (2 * m)
                        start = 2 * S - 2 * S // m
                        decay = a_t[:, prev, start:start + 2 * nb].rearrange("p (b u) -> p b u", u=2)
                        q = a_q[:, prev].rearrange("p (b u m) -> p b u m", u=2, m=m)[:, :, 1, :]
                        k = a_k[:, prev].rearrange("p (b u m) -> p b u m", u=2, m=m)[:, :, 0, :]
                        nc.vector.tensor_tensor(q, q, decay[:, :, 0].unsqueeze(2).to_broadcast([P, nb, m]), ALU.mult)
                        nc.vector.tensor_tensor(k, k, decay[:, :, 1].unsqueeze(2).to_broadcast([P, nb, m]),
                                                ALU.mult).then_inc(upd, 1)

                    def keep(g):
                        if g == 0:
                            ins = nc.vector.copy_predicated(a_sd.rearrange("p t c -> p (t c)"), a_mask[:, 0:S],
                                                            score[0][:])
                        else:
                            m = 1 << (g - 1)
                            to = a_sd.rearrange("p t (b u m) -> p (t b) u m", u=2, m=m)[:, :, 1, :]
                            mask = a_mask[:, S + (g - 1) * 256:S + g * 256].rearrange("p (b m) -> p b m", m=m)
                            of = score[g % 2][:, 0:256].rearrange("p (b m) -> p b m", m=m)
                            ins = nc.vector.copy_predicated(to, mask, of)
                        ins.then_inc(sd_done, 1)

                    def o_norm():
                        dve.wait_ge(sq_done, h + 1)
                        nc.vector.tensor_reduce(a_ss[:, 0], a_sq, AX, ALU.add).then_inc(oms_done, 1)
                        dve.wait_ge(oroot_done, h + 1)
                        nc.vector.reciprocal(a_ss[:, 2], a_ss[:, 1]).then_inc(rs_done, 1)
                        dve.wait_ge(rs_done, h + 1)
                        if later:
                            dve.wait_ge(oT_ready, h)
                        nc.vector.tensor_tensor(a_on, obank[:].rearrange("p (t c) -> p t c", t=TT),
                                                a_ss[:, 2].unsqueeze(2).to_broadcast([P, TT, P]),
                                                ALU.mult).then_inc(on_done, 1)

                    def into_y():
                        dve.wait_ge(oT_ready, h)
                        nc.vector.scalar_tensor_tensor(y[:, i - 2], turn[1][:], vec[:, 16 + idx:17 + idx],
                                                       a_gate[:, par], ALU.mult, ALU.mult).then_inc(y_done, 1)

                    if mix:
                        gate()
                    for g in range(8):
                        if mix:
                            move_on(g)
                            keep(g)
                        if g == 0 and end:
                            into_y()
                        if g == 3 and proj:
                            forget()
                        if g == 6 and proj:
                            query()
                        if g >= 4 and proj:
                            decays({4: (0,), 5: (1, 2), 6: (3, 4), 7: (5, 6)}[g])
                    if mix:
                        move_on(8)
                        o_norm()

                iterations(dve, body)

            def layer_b(n):
                B0 = ACC0[n]
                dve.wait_ge(s_dist, 16)

                def body(j, par, proj, mix, end):
                    i = j * 2 + par
                    h = i - 1
                    prev = 1 - par
                    later = not static(h) or h > 0

                    def unit(v):
                        u = b_unit(v)
                        bank = acc[(par + v) % 2]
                        dve.wait_ge(u_act, i * 12 + (u + 1))
                        if mix and u % 4 == 0:
                            dve.wait_ge(qkT_ready, h * 6 + (2 * (u // 4) + 2))
                        nc.vector.tensor_copy(b_raw[:, u], bank[:, 0:256])
                        if u == 0 and not (static(i) and i == 0):
                            dve.wait_ge(broot_done, i)
                        nc.vector.tensor_reduce(b_ss[:, u * 4:u * 4 + 4], b_sq.rearrange("p (c d) -> p c d", c=4),
                                                AX, ALU.add).then_inc(u_dve, 1)

                    def gate():
                        dve.wait_ge(eg_done, i + 1)
                        nc.vector.tensor_scalar(b_eg, b_eg, 1.0, None, ALU.add).then_inc(bg_step, 1)
                        dve.wait_ge(bg_step, i * 2 + 1)
                        nc.vector.reciprocal(b_eg, b_eg).then_inc(bg_step, 1)
                        dve.wait_ge(bg_step, i * 2 + 2)
                        nc.vector.tensor_tensor(b_gate[:, par], acc[par][:], b_eg, ALU.mult).then_inc(bgate_done, 1)

                    def norm_qk():
                        dve.wait_ge(broot_done, h + 1)
                        nc.vector.reciprocal(b_rs, b_rs).then_inc(brs_done, 1)
                        dve.wait_ge(brs_done, h + 1)
                        for g in range(3):
                            q = b_raw[:, g * 4:g * 4 + 4].rearrange("p t (c d) -> p (t c) d", c=4)
                            r = b_rs[:, g * 16:g * 16 + 16].unsqueeze(2).to_broadcast([P, 16, 64])
                            nc.vector.tensor_tensor(q, q, r, ALU.mult).then_inc(qn_done, 1)

                    def bias(a):
                        e, t = divmod(a, TT)
                        dve.wait_ge(s_ready, h * 8 + (a + 1))
                        if a >= 2 or later:
                            dve.wait_ge(pT_ready, h * 8 + (a - 1))
                        parts = ((slice(0, S), b_dist[:, t * S:(t + 1) * S], score[0][:]),
                                 (slice(S, S + P), b_dist[:, TT * S:TT * S + P], score[1][:, 0:P]),
                                 (slice(S + P, S + 2 * P), b_dist[:, TT * S + P:], score[1][:, P:2 * P]))
                        for g, (to, dist, of) in enumerate(parts):
                            last = nc.vector.scalar_tensor_tensor(b_s[:, a % 2, to], dist,
                                                                  slope[:, bass.ds(h * 2 + (16 * g + e), 1)], of,
                                                                  ALU.mult, ALU.add)
                        last.then_inc(s_biased, 1)
                        dve.wait_ge(s_biased, h * 8 + (a + 1))
                        nc.vector.tensor_reduce(b_small[:, 0, a % 2:a % 2 + 1], b_s[:, a % 2], AX, ALU.max,
                                                negate=True).then_inc(m_done, 1)

                    def p_out(a):
                        dve.wait_ge(pT_ready, h * 8 + (a + 1))
                        if a >= 2 or later:
                            dve.wait_ge(bo_ready, h * 8 + (a - 1))
                        nc.vector.tensor_copy(b_pt[:, a % 2, S:], turn[1][:, 0:256]).then_inc(pT_dve, 1)

                    def o_out(a):
                        e, t = divmod(a, TT)
                        dve.wait_ge(e_done, h * 8 + (a + 1))
                        nc.vector.reciprocal(b_small[:, 2, a % 2:a % 2 + 1],
                                             b_small[:, 1, a % 2:a % 2 + 1]).then_inc(l_done, 1)
                        dve.wait_ge(l_done, h * 8 + (a + 1))
                        dve.wait_ge(bo_ready, h * 8 + (a + 1))
                        if a == 0 and later:
                            dve.wait_ge(boT_ready, h)
                        nc.vector.tensor_scalar(b_o[:, t, e * 64:(e + 1) * 64], (obank, spare)[a % 2][:, 0:64],
                                                b_small[:, 2, a % 2:a % 2 + 1], None, ALU.mult).then_inc(bo_done, 1)

                    def into_y():
                        dve.wait_ge(boT_ready, h + 1)
                        split = "p (r q a) -> p r q a"
                        nc.vector.tensor_tensor(y[:, h].rearrange("p (a q r) -> p r q a", q=4, r=4),
                                                turn[0][:].rearrange(split, r=4, q=4),
                                                b_gate[:, prev].rearrange(split, r=4, q=4), ALU.mult).then_inc(y_done, 1)

                    plan = []
                    if proj:
                        for v in range(B_UNITS + 1):
                            plan.append((8 * v + 8.5, gate if v == 4 else lambda v=v: unit(v)))
                    if mix:
                        plan.append((0, norm_qk))
                        for a in range(B_STEPS):
                            plan.append((16 + 9 * a + 2, lambda a=a: bias(a)))
                            plan.append((16 + 9 * a + 10.4, lambda a=a: p_out(a)))
                            plan.append((16 + 9 * a + 19, lambda a=a: o_out(a)))
                        plan.append((103.5, into_y))
                    for _, step in sorted(plan, key=lambda p: p[0]):
                        step()

                iterations(dve, body)

            def layer_c(n):
                dve.wait_ge(s_cvec, 80)
                nc.vector.tensor_tensor(c_ws, c_ws, causal.unsqueeze(1).to_broadcast([P, HEADS, P]),
                                        ALU.mult).then_inc(cw_masked, 1)

                def gelu(u, bank, width, to):
                    dve.wait_ge(sqc_done, u + 1)
                    if u >= 2:
                        dve.wait_ge(gelu_done, u - 1)
                    z = c_z[:, u % 2, 0:width]
                    nc.vector.tensor_scalar(z, c_x2[:, u % 2, 0:width], 0.044715, 1.0,
                                            ALU.mult, ALU.add).then_inc(poly_done, 1)
                    dve.wait_ge(poly_done, u + 1)
                    nc.vector.tensor_tensor(z, z, bank, ALU.mult).then_inc(z_done, 1)
                    dve.wait_ge(sig_done, u + 1)
                    nc.vector.tensor_tensor(to, z, bank, ALU.mult).then_inc(gelu_done, 1)

                def statistics():
                    for t in range(TT):
                        for half in range(2):
                            last = nc.vector.bn_stats(c_st[:, t, half * 6:half * 6 + 6],
                                                      c_v[:, t, half * 512:(half + 1) * 512])
                        last.then_inc(cstat_done, 1)
                        dve.wait_ge(cstat_done, t + 1)
                        nc.vector.bn_aggr(c_mv[:, t, 0:2], c_st[:, t]).then_inc(cms_done, 1)
                def layer_norm(ts):
                    for t in ts:
                        dve.wait_ge(croot_done, t + 1)
                        nc.vector.reciprocal(c_mv[:, t, 3:4], c_mv[:, t, 2:3]).then_inc(ln_step, 1)
                        dve.wait_ge(ln_step, 3 * t + 1)
                        nc.vector.tensor_scalar(c_v[:, t], c_v[:, t], c_mv[:, t, 0:1], c_mv[:, t, 3:4],
                                                ALU.subtract, ALU.mult).then_inc(ln_step, 1)
                        dve.wait_ge(ln_step, 3 * t + 2)
                        nc.vector.tensor_tensor(c_v[:, t], c_v[:, t], c_vw, ALU.mult).then_inc(ln_step, 1)
                        dve.wait_ge(ln_step, 3 * t + 3)
                        nc.vector.tensor_tensor(c_v[:, t], c_v[:, t], c_vb, ALU.add).then_inc(ln_done, 1)

                def gated(g):
                    dve.wait_ge(sp_ready, g + 1)
                    nc.vector.tensor_tensor(y[:, g], y[:, g], score[g % 2][:], ALU.mult).then_inc(y_done, 1)

                for u in range(16):
                    p, t = divmod(u, TT)
                    gelu(u, acc[u % 2][:, 0:256], 256, c_v[:, t, p * 256:(p + 1) * 256])
                dve.wait_ge(gelu_done, 16)
                statistics()
                for g in range(HEADS):
                    gelu(16 + g, acc[0][:], S, y[:, g])
                    dve.wait_ge(cg_act, g + 1)
                    nc.vector.tensor_tensor(c_g[:, 1], c_g[:, 0], acc[1][:], ALU.mult).then_inc(cgate_done, 1)
                    dve.wait_ge(cgate_done, g + 1)
                    nc.vector.tensor_tensor(y[:, g], y[:, g], c_g[:, 1], ALU.mult).then_inc(cug_done, 1)
                    dve.wait_ge(cug_done, g + 1)
                    layer_norm(((0, 1), (2, 3))[g] if g < 2 else ())
                    if g >= 3:
                        gated(g - 3)
                for g in range(5, HEADS):
                    gated(g)

            nc.vector.memset(ones[:], 1.0)
            nc.vector.memset(eps[:], EPS).then_inc(s_set, 1)
            norm(0)
            bounds()
            for n in range(layers):
                if n:
                    norm(n)
                if n % 3 == 0:
                    layer_a(n, n // 3)
                elif n == 1:
                    layer_b(n)
                else:
                    layer_c(n)
                for k in range(KT):
                    split_y(n, k)
                residual(n)


_INPUTS = ("x", "norm_w", "a_w_in", "a_lower_bounds", "a_o_norm_w", "a_w_out", "b_w_in", "b_q_norm_w",
           "b_k_norm_w", "b_w_out", "c_w_in", "c_v_norm_w", "c_v_norm_b", "c_w_s", "c_b_s", "c_w_out")


def kernel(**inputs):
    import concourse.bacc as bacc
    from concourse.bass_utils import run_bass_kernel_spmd

    nc = bacc.Bacc("TRN2", target_bir_lowering=False, num_devices=1)
    arrays = {f"in_{name}": np.ascontiguousarray(inputs[name]) for name in _INPUTS}
    arrays.update(shape_constants())
    args = [nc.dram_tensor(name, a.shape, mybir.dt.from_np(a.dtype), kind="ExternalInput").ap()
            for name, a in arrays.items()]
    result = nc.dram_tensor("out_0", (1, S, D), F32, kind="ExternalOutput").ap()
    build(nc, *args, result)
    r = run_bass_kernel_spmd(nc, [arrays], core_ids=[0])
    return r.results[0]["out_0"]
```

```python
from contextlib import ExitStack

import numpy as np

import concourse.bass as bass
from concourse import mybir

F32 = mybir.dt.float32
F32R = mybir.dt.float32r
U8 = mybir.dt.uint8
ALU = mybir.AluOpType
ACT = mybir.ActivationFunctionType
AX = mybir.AxisListType.X

P = 128
D = 1024
S = 512
KT = D // P
TT = S // P
HEADS = D // P
EPS = 1e-6
LB_FLOOR = 1e-30

RAW = 4
HALF = 3
SLOTS = 2 * HALF + 1
A_PARTS = (1, 0, 2, 3)
B_PARTS = (0, 1, 2, 9, 3, 4, 5, 6, 7, 8)
A_CHUNKS, B_CHUNKS, OUT_CHUNKS = len(A_PARTS), len(B_PARTS), 8
OUT_RING = (0, 1, 3, 4, 2, 5, 6, 4)
OUT_COLUMNS = (0, 1, 2, 3, 4, 5, 7, 6)
WIDE = 4
NARROW = ((0, 0), (0, 1), (1, 0), (1, 1), (0, 2), (1, 2), (0, 3), (1, 3))
OUT_UNITS = WIDE + len(NARROW)
FINAL = tuple(WIDE + 1 + NARROW.index((1, t)) for t in range(4))
C_V_CHUNKS, C_UG_CHUNKS = 8, 16
LEVELS = 7
G_STEPS = LEVELS + 3

SMALL_CONSTANTS = 8
GELU_SCALE = 2 * (2 / np.pi) ** 0.5
MASKED = -3e38
DIL = (1, 4, 16)
WINDOW = (128, 512, 2048)
B_UNITS = 12
B_STEPS = 8
QK_TURNS = (8, 9, 11, 12, 14, 15)
SLOT, SLOT_STEP = 17, 9

LAYER_IN = (HEADS * A_CHUNKS, HEADS * B_CHUNKS, C_V_CHUNKS + C_UG_CHUNKS, HEADS * A_CHUNKS)
IN0 = [sum(LAYER_IN[:n]) + OUT_CHUNKS * n for n in range(4)]
OUT0 = [IN0[n] + LAYER_IN[n] for n in range(4)]

ACC_OF = (HEADS * A_CHUNKS, HEADS * (B_UNITS + 1), 4 * TT + C_UG_CHUNKS, HEADS * A_CHUNKS)
ACC0 = [sum(ACC_OF[:n]) for n in range(4)]


def a_ring(par, c):
    return c // 2 * HALF + c % 2


def b_half(par, g):
    return (par + g) % 2


def b_ring(par, c):
    if c == 3:
        return SLOTS - 1
    g, part = divmod(c if c < 3 else c - 1, 3)
    return b_half(par, g) * HALF + part


def b_unit(v):
    return v if v < 4 else v - 1


def pair_ring(c):
    return c // 2 % 2 * HALF + c % 2


def c_ring(c):
    last = C_V_CHUNKS + C_UG_CHUNKS - 2
    return pair_ring(c) if c < last else (2, 5)[c - last]


def shape_constants():
    ident = np.eye(P, dtype=np.float32)
    a, q, r = np.meshgrid(np.arange(8), np.arange(4), np.arange(4), indexing="ij")
    perm = np.zeros((P, P), np.float32)
    perm[(16 * a + 4 * q + r).ravel(), (32 * r + 8 * q + a).ravel()] = 1
    s = np.arange(P)[:, None]
    masks = np.zeros((P, P * TT + LEVELS * 64 * TT), np.float32)
    masks[:, :P * TT] = np.tile(np.eye(P, dtype=np.float32), (1, TT))
    for n in range(LEVELS):
        m = 1 << n
        u = np.arange(64)
        t = (u // m) * 2 * m + m + u % m
        own = (s // (2 * m) == t // (2 * m)) & (s % (2 * m) < m)
        at = P * TT + n * 64 * TT
        masks[:, at:at + 64 * TT] = np.tile(own.astype(np.float32), (1, TT))
    p = np.arange(S)
    token = 16 * (p % 32) + 4 * (p // 32 % 4) + p // 128
    dist = token[:, None] - token[None, :]
    near = np.where((dist >= 0) & (dist <= WINDOW[0]), -dist, MASKED).astype(np.float32)
    own = dist[:P, :P]
    dil4 = np.where(own >= 0, -own, MASKED).astype(np.float32)
    dil16 = np.where((own >= 0) & (own % DIL[2] == 0), -own, MASKED).astype(np.float32)
    negdist = np.concatenate([near.reshape(TT, P, S).transpose(1, 0, 2).reshape(P, TT * S), dil4, dil16], 1)
    n = np.arange(1, 49, dtype=np.float32)
    slopes = np.tile(np.exp2(-8.0 * n / 48).astype(np.float32), (P, 1))
    causal = (np.arange(P)[:, None] >= np.arange(P)[None, :]).astype(np.float32)
    return {"c_ident": ident, "c_perm": perm, "c_masks": masks,
            "c_negdist": np.ascontiguousarray(negdist), "c_slopes": slopes, "c_causal": causal}


def build(nc, x, norm_w, a_w_in, a_lower_bounds, a_o_norm_w, a_w_out, b_w_in, b_q_norm_w, b_k_norm_w,
          b_w_out, c_w_in, c_v_norm_w, c_v_norm_b, c_w_s, c_b_s, c_w_out,
          c_ident, c_perm, c_masks, c_negdist, c_slopes, c_causal, out, layers=4):
    ctx = ExitStack()

    def sb(name, shape, dt=F32):
        return ctx.enter_context(nc.sbuf_tensor(name, shape, dt))

    def sem(name):
        return ctx.enter_context(nc.semaphore(name))

    with ctx:
        xt = sb("xt", [P, TT, D])
        op_hi = sb("op_hi", [P, KT, S], F32R)
        op_lo = sb("op_lo", [P, KT, S], F32R)
        y = sb("y", [P, KT, S])
        raw = sb("raw", [P, RAW, KT, P])
        w_hi = sb("w_hi", [P, SLOTS, KT, P], F32R)
        w_lo = sb("w_lo", [P, SLOTS, KT, P], F32R)
        xn = y[:, 0:4].rearrange("p (a b) c -> p a (b c)", a=2)
        norm_b = y[:, 4:6].rearrange("p b c -> p (b c)")
        ident = sb("ident", [P, P])
        perm = sb("perm", [P, P])
        stat = sb("stat", [P, 16])
        eps = sb("eps", [P, 1])
        vec_rows = sb("vec_rows", [24, P])
        vec = sb("vec", [P, 24])
        bound = sb("bound", [P, 5, 2, HEADS])
        scratch = sb("scratch", [P, 17008])

        def carve(start, *shape):
            n = int(np.prod(shape))
            assert start + n <= 17008
            v = scratch[:, start:start + n]
            if len(shape) == 2:
                v = v.rearrange("p (a b) -> p a b", a=shape[0])
            if len(shape) == 3:
                v = v.rearrange("p (a b c) -> p a b c", a=shape[0], b=shape[1])
            return v, start + n

        at = 0
        a_q, at = carve(at, 2, S)
        a_k, at = carve(at, 2, S)
        a_t, at = carve(at, 2, 2 * S)
        a_v, at = carve(at, 2, S)
        a_gate, at = carve(at, 2, S)
        a_sig, at = carve(at, 3, S)
        a_vt, at = carve(at, TT, P)
        a_sd, at = carve(at, TT, P)
        a_sx, at = carve(at, 6, P)
        a_sq, at = carve(at, TT, P)
        a_on, at = carve(at, TT, P)
        a_ss, at = carve(at, 3, TT)
        a_qk, at = carve(at, S + S // 2)
        qk_hi, qk_lo = (w[:, 2, 0:6].rearrange("p k c -> p (k c)") for w in (w_hi, w_lo))
        ones_sq = w_hi[:, 5, 0]
        mask_f, at = carve(at, TT * P + LEVELS * TT * 64)
        a_mask = sb("a_mask", [P, TT * P + LEVELS * TT * 64], U8)
        at = 0
        b_raw, at = carve(at, B_UNITS, 256)
        b_qk, at = carve(at, 6, S)
        b_v, at = carve(at, 2, B_UNITS, P)
        b_gate, at = carve(at, 2, S)
        b_eg, at = carve(at, S)
        b_sq, at = carve(at, 256)
        b_s, at = carve(at, 2, 768)
        b_pt, at = carve(at, 2, 768)
        b_dist, at = carve(at, TT * S + 256)
        b_o, at = carve(at, TT, P)
        b_ss, at = carve(at, B_UNITS * 4)
        b_rs, at = carve(at, B_UNITS * 4)
        b_small, at = carve(at, 4, 2)
        slope = sb("slope", [P, 48])
        at = 0
        c_v, at = carve(at, TT, D)
        c_vw, at = carve(at, D)
        c_vb, at = carve(at, D)
        c_ws, at = carve(at, HEADS, P)
        c_wt, at = carve(at, HEADS, P)
        c_bs, at = carve(at, HEADS, P)
        c_sp, at = carve(at, S)
        c_x2, at = carve(at, 2, S)
        c_z, at = carve(at, 2, S)
        c_g, at = carve(at, 2, S)
        c_st, at = carve(at, TT, 12)
        c_mv, at = carve(at, TT, 4)
        causal, at = carve(at, P)

        ps = [ctx.enter_context(nc.psum_tensor(f"ps{n}", [P, S], F32)) for n in range(8)]
        acc = ps[0:2]
        score = ps[2:4]
        turn = ps[4:6]
        obank = ps[6]
        spare = ps[7]

        s_ident = sem("s_ident")
        s_const = sem("s_const")
        s_mask = sem("s_mask")
        s_dist = sem("s_dist")
        s_x = [sem(f"s_x{t}") for t in range(TT)]
        s_normw = sem("s_normw")
        raw_landed = [sem(f"raw_landed{n}") for n in range(RAW)]
        hi_done = sem("hi_done")
        lo_done = sem("lo_done")
        s_vecT = sem("s_vecT")
        s_bact = sem("s_bact")
        bound_step = sem("bound_step")
        vec_step = sem("vec_step")
        rstd_done = sem("rstd_done")
        sd_zero = sem("sd_zero")
        s_set = sem("s_set")
        ssq_done = sem("ssq_done")
        ms_done = sem("ms_done")
        root_done = sem("root_done")
        xn_done = sem("xn_done")
        xT_done = sem("xT_done")
        h_hi = sem("h_hi")
        h_lo = sem("h_lo")
        x_new = sem("x_new")
        out_ready = sem("out_ready")
        y_done = sem("y_done")
        y_hi = sem("y_hi")
        y_lo = sem("y_lo")
        acc_ready = sem("acc_ready")
        s_out = sem("s_out")
        f_act = sem("f_act")
        q_act = sem("q_act")
        v_act = sem("v_act")
        g_act = sem("g_act")
        kf_done = sem("kf_done")
        qf_done = sem("qf_done")
        qk_done = sem("qk_done")
        qk_hi_done = sem("qk_hi_done")
        qk_lo_done = sem("qk_lo_done")
        q_done = sem("q_done")
        gate_done = sem("gate_done")
        vT_ready = sem("vT_ready")
        vT_done = sem("vT_done")
        g_ready = sem("g_ready")
        sd_done = sem("sd_done")
        sx_done = sem("sx_done")
        upd = sem("upd")
        t_step = sem("t_step")
        rs_done = sem("rs_done")
        o_ready = sem("o_ready")
        sq_done = sem("sq_done")
        oms_done = sem("oms_done")
        oroot_done = sem("oroot_done")
        on_done = sem("on_done")
        oT_ready = sem("oT_ready")
        u_act = sem("u_act")
        u_dve = sem("u_dve")
        bms_done = sem("bms_done")
        broot_done = sem("broot_done")
        qn_done = sem("qn_done")
        qkT_ready = sem("qkT_ready")
        qkT_done = sem("qkT_done")
        s_ready = sem("s_ready")
        s_biased = sem("s_biased")
        m_done = sem("m_done")
        e_done = sem("e_done")
        pT_ready = sem("pT_ready")
        pT_act = sem("pT_act")
        pT_dve = sem("pT_dve")
        bo_ready = sem("bo_ready")
        bo_done = sem("bo_done")
        boT_ready = sem("boT_ready")
        eg_done = sem("eg_done")
        bg_step = sem("bg_step")
        brs_done = sem("brs_done")
        l_done = sem("l_done")
        bgate_done = sem("bgate_done")
        s_cvec = sem("s_cvec")
        cw_masked = sem("cw_masked")
        cwT_ready = sem("cwT_ready")
        cwT_done = sem("cwT_done")
        sqc_done = sem("sqc_done")
        z_done = sem("z_done")
        sig_done = sem("sig_done")
        gelu_done = sem("gelu_done")
        cms_done = sem("cms_done")
        croot_done = sem("croot_done")
        ln_done = sem("ln_done")
        sp_ready = sem("sp_ready")
        sp_done = sem("sp_done")
        poly_done = sem("poly_done")
        cstat_done = sem("cstat_done")
        ln_step = sem("ln_step")
        cg_act = sem("cg_act")
        cgate_done = sem("cgate_done")
        cug_done = sem("cug_done")

        block = ctx.enter_context(nc.Block())

        def landed(n0, per, j, par, c):
            n = n0 + per * par + c
            return n % RAW, 16 * (n // RAW + 1) + 16 * (2 * per // RAW) * j

        def chunk(n0, per, j, par, c):
            return n0 + per * par + c + 2 * per * j

        def columns(w, col):
            return w[:, bass.ds(col, P)].rearrange("(k p) c -> p k c", p=P)

        def static(v):
            return isinstance(v, int)

        def iterations(eng, body, peeled=0):
            body(0, 0, True, False, False)
            body(0, 1, True, True, False)
            with eng.Fori(1, HEADS // 2 - peeled) as j:
                body(j, 0, True, True, True)
                body(j, 1, True, True, True)
            for j in range(HEADS // 2 - peeled, HEADS // 2):
                body(j, 0, True, True, True)
                body(j, 1, True, True, True)
            body(HEADS // 2, 0, False, True, True)
            body(HEADS // 2, 1, False, False, True)

        def terms(a, b):
            return ((a[0], b[0]), (a[1], b[0]), (a[0], b[1]))

        def h_part(buf, n, t, half):
            ks = slice(half * 4, half * 4 + 4)
            if n == 1:
                return buf[:, ks].rearrange("p k (r a) -> p k r a", a=32)[:, :, :, 8 * t:8 * t + 8]
            return buf[:, ks, t * P:(t + 1) * P]

        def turned_part(n, t, half):
            bank = h_banks(n, t)[half][:]
            if n == 1:
                return bank.rearrange("p (k r a) -> p k r a", k=4, a=8)
            return bank.rearrange("p (k c) -> p k c", k=4)

        def h_banks(n, t):
            if t == 1:
                return score
            if t == 2:
                return (obank, spare)
            return acc if t == 3 and n == 1 else turn

        def wide_bank(n, t):
            return acc[t] if t < 2 else ((obank, spare) if n == 2 else score)[t - 2]

        def v_bank(u):
            return (acc[0], acc[1], score[0], score[1])[u % 4][:, 0:256]

        @block.sync
        def _(sp):
            def load(slot, src, n):
                if static(n):
                    if n >= RAW:
                        sp.wait_ge(lo_done, n - (RAW - 1))
                    sp.dma_start(raw[:, slot], src).then_inc(raw_landed[slot], 16)
                else:
                    split = sp.to_reg(n - (RAW - 1))
                    sp.dma_start(raw[:, slot], src).wait_op(lo_done, split, "sem-ge").then_inc(raw_landed[slot], 16)

            def load_columns(n0, w, cols):
                for c, col in enumerate(cols):
                    load((n0 + c) % RAW, columns(w, col), n0 + c)

            def load_layer(n, w, parts):
                per = len(parts)

                def body(j, par, proj, mix, end):
                    if proj:
                        for c, part in enumerate(parts):
                            col = j * (2 * P) + (part * D + par * P)
                            if not static(col):
                                col = sp.snap(col)
                            load(landed(IN0[n], per, j, par, c)[0], columns(w, col), chunk(IN0[n], per, j, par, c))
                iterations(sp, body)

            sp.dma_start(xt[:, 0], x[0, 0:P, :]).then_inc(s_x[0], 16)
            sp.dma_start(norm_b, norm_w[0:1, :].to_broadcast([P, D])).then_inc(s_normw, 16)
            for t in range(1, TT):
                sp.dma_start(xt[:, t], x[0, t * P:(t + 1) * P, :]).then_inc(s_x[t], 16)
            for n in range(layers):
                w_out = (a_w_out, b_w_out, c_w_out, a_w_out)[n][n // 3]
                if n:
                    sp.wait_ge(y_lo, KT * n)
                    sp.dma_start(norm_b, norm_w[n:n + 1, :].to_broadcast([P, D])).then_inc(s_normw, 16)
                if n % 3 == 0:
                    load_layer(n, a_w_in[n // 3], A_PARTS)
                if n == 1:
                    sp.wait_ge(y_done, KT)
                    sp.dma_start(b_dist, c_negdist).then_inc(s_dist, 16)
                    load_layer(n, b_w_in[0], B_PARTS)
                if n == 2:
                    sp.wait_ge(y_done, 2 * KT)
                    sp.dma_start(causal, c_causal).then_inc(s_cvec, 16)
                    sp.dma_start(c_ws, c_w_s[0].rearrange("g t s -> t g s")).then_inc(s_cvec, 16)
                    sp.dma_start(c_vw, c_v_norm_w[0:1, :].to_broadcast([P, D])).then_inc(s_cvec, 16)
                    sp.dma_start(c_vb, c_v_norm_b[0:1, :].to_broadcast([P, D])).then_inc(s_cvec, 16)
                    sp.dma_start(c_bs, c_b_s[0:1].to_broadcast([P, HEADS, P])).then_inc(s_cvec, 16)
                    load_columns(IN0[n], c_w_in[0], [D + c * P for c in range(C_V_CHUNKS)])
                    load_columns(IN0[n] + C_V_CHUNKS, c_w_in[0],
                                 [part * D + g * P for g in range(HEADS) for part in (0, 2)])
                load_columns(OUT0[n], w_out, [c * P for c in OUT_COLUMNS])
            for t in range(TT):
                sp.wait_ge(x_new, (layers - 1) * OUT_UNITS + FINAL[t])
                sp.dma_start(out[0, t * P:(t + 1) * P, :], xt[:, t]).then_inc(s_out, 16)
            sp.wait_ge(s_out, 16 * TT)

        @block.gpsimd
        def _(pool):
            pool.dma_start(ident[:], c_ident).then_inc(s_ident, 16)
            pool.dma_start(vec_rows[0:16, :], a_lower_bounds.rearrange("l (h p) -> (l h) p", p=P)).then_inc(s_const, 16)
            pool.dma_start(vec_rows[16:18, :], a_o_norm_w).then_inc(s_const, 16)
            for e in range(2):
                pool.dma_start(vec_rows[18:21, e * 64:(e + 1) * 64], b_q_norm_w[0]).then_inc(s_const, 16)
                pool.dma_start(vec_rows[21:24, e * 64:(e + 1) * 64], b_k_norm_w[0]).then_inc(s_const, 16)
            pool.dma_start(mask_f, c_masks).then_inc(s_mask, 16)
            pool.dma_start(perm[:], c_perm).then_inc(s_const, 16)
            pool.dma_start(slope[:], c_slopes).then_inc(s_const, 16)

            def split_lo(slot, ring, n):
                pool.wait_ge(hi_done, n + 1)
                nc.gpsimd.tensor_tensor(w_lo[:, ring], raw[:, slot], w_hi[:, ring].bitcast(F32),
                                        ALU.subtract).then_inc(lo_done, 1)

            def split_layer(n, per, rings):
                def body(j, par, proj, mix, end):
                    if proj:
                        for c in range(per):
                            split_lo(landed(IN0[n], per, j, par, c)[0], rings(par, c), chunk(IN0[n], per, j, par, c))
                iterations(pool, body)

            for n in range(layers):
                if n % 3 == 0:
                    split_layer(n, len(A_PARTS), a_ring)
                elif n == 1:
                    split_layer(n, len(B_PARTS), b_ring)
                else:
                    for c in range(LAYER_IN[n]):
                        split_lo((IN0[n] + c) % RAW, c_ring(c), IN0[n] + c)
                for c in range(OUT_CHUNKS):
                    split_lo((OUT0[n] + c) % RAW, OUT_RING[c], OUT0[n] + c)

        @block.tensor
        def _(pe):
            def feature_step(bank, ring, k, tokens=slice(0, S)):
                w = (w_hi[:, ring, k, :], w_lo[:, ring, k, :])
                h = (op_hi[:, k, tokens], op_lo[:, k, tokens])
                for p, (a, b) in enumerate(terms(w, h)):
                    last = nc.tensor.matmul(bank, a, b, start=(k == 0 and p == 0), stop=(k == KT - 1 and p == 2))
                return last

            def token_step(bank, slots, k, t):
                if isinstance(slots, slice):
                    w = (w_hi[:, slots, k, :], w_lo[:, slots, k, :])
                else:
                    w = tuple(half[:, 0:2 * HALF].rearrange("p (h s) k c -> p h s k c", h=2)[:, :, 0:2, k, :]
                              for half in (w_hi, w_lo))
                h = (op_hi[:, k, t * P:(t + 1) * P], op_lo[:, k, t * P:(t + 1) * P])
                for p, (a, b) in enumerate(terms(h, w)):
                    last = nc.tensor.matmul(bank, a, b, start=(k == 0 and p == 0), stop=(k == KT - 1 and p == 2))
                return last

            def transpose_x(n, t):
                if n == 0 and t == 0:
                    pe.wait_ge(s_ident, 16)
                turned = perm if n == 1 else ident
                for half in range(2):
                    pe.wait_ge(xn_done, 8 * n + 2 * t + half + 1)
                    bank = h_banks(n, t)[half]
                    if t == 3 and n != 1:
                        pe.wait_ge(h_lo, 8 * n + 1 + half)
                    for k in range(4):
                        kk = half * 4 + k
                        last = nc.tensor.transpose(bank[:, k * P:(k + 1) * P],
                                                   xn[:, t % 2, kk * P:(kk + 1) * P], turned[:])
                    last.then_inc(xT_done, 1)

            def wide(n, k, tiles):
                pe.wait_ge(y_lo, KT * n + k + 1)
                if k == 0:
                    pe.wait_ge(lo_done, OUT0[n] + 4)
                for t in tiles:
                    last = token_step(wide_bank(n, t)[:], None, k, t)
                    if k == KT - 1:
                        last.then_inc(out_ready, 1)

            def output_projection(n):
                wide(n, KT - 1, range(TT))
                for u, (b, t) in enumerate(NARROW, WIDE):
                    if t == 0:
                        pe.wait_ge(lo_done, OUT0[n] + 6 + 2 * b)
                    pe.wait_ge(x_new, OUT_UNITS * n + (u - WIDE + 1 if u < WIDE + 2 else u - 1))
                    for k in range(KT):
                        last = token_step(acc[u % 2][:, 0:256], (slice(2, 6, 3), slice(4, 7, 2))[b], k, t)
                    last.then_inc(out_ready, 1)
                    if n + 1 < layers and u in (8, 9):
                        transpose_x(n + 1, u - 8)

            def lead_in(n):
                transpose_x(n, 2)
                for c in range(2):
                    if n % 3 == 0:
                        pe.wait_ge(h_lo, 8 * n + 4)
                        if n:
                            pe.wait_ge(x_new, OUT_UNITS * n - 1 + c)
                        pe.wait_ge(lo_done, IN0[n] + c + 1)
                        for k in range(KT):
                            feature_step(acc[c][:, 0:256], a_ring(0, c), k, slice(0, 256))
                    elif n == 2:
                        v_unit(n, 0, c)
                    if c == 0:
                        transpose_x(n, 3)
                if n == 0:
                    pe.wait_ge(h_lo, 6)
                    pe.wait_ge(s_const, 16 * SMALL_CONSTANTS)
                    nc.tensor.transpose(spare[:, 0:24], vec_rows[:], ident[0:24, 0:24]).then_inc(s_vecT, 1)
                if n != 2:
                    pe.wait_ge(h_lo, 8 * n + 8)

            def v_unit(n, p, t):
                u = 4 * p + t
                bank = v_bank(u)
                if p == 0:
                    pe.wait_ge(lo_done, IN0[n] + 2)
                    pe.wait_ge(h_lo, 8 * n + 2 * t + 2)
                if u < 2:
                    pe.wait_ge(x_new, OUT_UNITS * n - 1 + u)
                elif u >= 4:
                    pe.wait_ge(gelu_done, u - 3)
                for k in range(KT):
                    last = token_step(bank, slice(p % 2 * HALF, p % 2 * HALF + 2), k, t)
                last.then_inc(acc_ready, 1)

            def layer_a(n, idx):
                H0 = HEADS * idx

                def body(j, par, proj, mix, end):
                    i = j * 2 + par
                    h = i + (H0 - 1)
                    prev = 1 - par
                    later = not static(h) or h > H0

                    def turn_v():
                        pe.wait_ge(v_act, h + 1)
                        if later:
                            pe.wait_ge(vT_done, h)
                        for t in range(TT):
                            last = nc.tensor.transpose(turn[0][:, t * P:(t + 1) * P],
                                                       a_v[:, prev, t * P:(t + 1) * P], ident[:])
                        last.then_inc(vT_ready, 1)

                    def scores(g):
                        q, k, bank = a_q[:, prev], a_k[:, prev], score[g % 2]
                        if g < 2:
                            pe.wait_ge(qk_lo_done, h + 1)
                        else:
                            pe.wait_ge(upd, h * 8 + (g - 1))
                        if g >= 2:
                            pe.wait_ge(sd_done, h * 8 + (g - 1))
                        elif later:
                            pe.wait_ge(sx_done, h * 2 + (g - 1))
                        if g < 2:
                            cols, to = (slice(0, S), bank[:]) if g == 0 else (slice(S, S + 256), bank[:, 0:256])
                            nc.tensor.matmul(to, ones_sq, qk_hi[:, cols], start=True, stop=False)
                            last = nc.tensor.matmul(to, ones_sq, qk_lo[:, cols], start=False, stop=True)
                        elif g <= LEVELS:
                            m = 1 << (g - 1)
                            upper = q.rearrange("p (t b u m) -> p t b u m", t=TT, u=2, m=m)
                            for t in range(TT):
                                last = nc.tensor.matmul(bank[:, t * 64:(t + 1) * 64], k[:, t * P:(t + 1) * P],
                                                        upper[:, t, :, 1, :], start=True, stop=True)
                        elif g == LEVELS + 1:
                            for s in (0, 2):
                                last = nc.tensor.matmul(bank[:, s * 64:s * 64 + P], k[:, s * P:(s + 1) * P],
                                                        q[:, (s + 1) * P:(s + 2) * P], start=True, stop=True)
                        else:
                            for s in (0, 1):
                                last = nc.tensor.matmul(bank[:, s * 256:(s + 1) * 256], k[:, s * P:(s + 1) * P],
                                                        q[:, 2 * P:4 * P], start=True, stop=True)
                        last.then_inc(g_ready, 1)

                    def values():
                        pe.wait_ge(sd_done, h * 8 + 8)
                        pe.wait_ge(sx_done, h * 2 + 2)
                        pe.wait_ge(vT_done, h + 1)
                        if later:
                            pe.wait_ge(on_done, h)
                        pairs = (((a_sd[:, 0], 0),),
                                 ((a_sd[:, 1], 1), (a_sx[:, 0], 0)),
                                 ((a_sd[:, 2], 2), (a_sx[:, 2], 0), (a_sx[:, 4], 1)),
                                 ((a_sd[:, 3], 3), (a_sx[:, 1], 2), (a_sx[:, 3], 0), (a_sx[:, 5], 1)))
                        for t in range(TT):
                            for c, (weights, s) in enumerate(pairs[t]):
                                last = nc.tensor.matmul(obank[:, t * P:(t + 1) * P], weights, a_vt[:, s],
                                                        start=(c == 0), stop=(c == len(pairs[t]) - 1))
                        last.then_inc(o_ready, 1)

                    def turn_o():
                        pe.wait_ge(on_done, h)
                        if not static(i) or i > 2:
                            pe.wait_ge(y_done, i + (KT * n - 2))
                        for t in range(TT):
                            last = nc.tensor.transpose(turn[1][:, t * P:(t + 1) * P], a_on[:, t], ident[:])
                        last.then_inc(oT_ready, 1)

                    def bank_free(c):
                        first = static(i) and i == 0
                        if c == 0 and not first:
                            pe.wait_ge(v_act, i + H0)
                        if c == 1 and not first:
                            pe.wait_ge(gate_done, i + H0)
                        if c == 2:
                            pe.wait_ge(f_act, i + (H0 + 1))
                        if c == 3:
                            pe.wait_ge(q_done, i + (H0 + 1))

                    steps = {}
                    if mix:
                        steps[1] = [turn_v]
                        for g in range(G_STEPS):
                            steps.setdefault(int(2 + 2.4 * g), []).append(lambda g=g: scores(g))
                        steps[27] = [values]
                    if end:
                        steps.setdefault(3, []).append(turn_o)
                    if mix and not proj:
                        for g in range(3, G_STEPS):
                            steps[int(2 + 2.4 * g)].append(lambda k=g - 3: wide(n, k, (0, 1)))
                        for k in range(KT - 3):
                            steps[27].append(lambda k=k: wide(n, k, (2, 3)))
                    if end and not mix:
                        for k in (KT - 3, KT - 2):
                            steps[3].append(lambda k=k: wide(n, k, (2, 3)))
                    for ks in range(len(A_PARTS) * KT):
                        c, k = divmod(ks, KT)
                        if proj and static(i) and i == 0 and c < 2:
                            last = feature_step(acc[c][:, 256:S], a_ring(par, c), k, slice(256, S))
                            if k == KT - 1:
                                last.then_inc(acc_ready, 1)
                        elif proj:
                            if k == 0:
                                pe.wait_ge(lo_done, chunk(IN0[n], len(A_PARTS), j, par, c) + 1)
                                bank_free(c)
                            last = feature_step(acc[c % 2][:], a_ring(par, c), k)
                            if k == KT - 1:
                                last.then_inc(acc_ready, 1)
                        for step in steps.get(ks, ()):
                            step()

                iterations(pe, body)

            def layer_b(n):
                def body(j, par, proj, mix, end):
                    i = j * 2 + par
                    h = i - 1
                    prev = 1 - par
                    later = not static(h) or h > 0

                    def turn_qk(b):
                        g, part = divmod(b, 2)
                        pe.wait_ge(qn_done, h * 3 + (g + 1))
                        if b >= 2:
                            pe.wait_ge(qkT_done, h * 6 + (b - 1))
                        elif later:
                            pe.wait_ge(y_done, h + KT * n)
                        for t in range(TT):
                            last = nc.tensor.transpose(turn[b % 2][:, t * P:(t + 1) * P],
                                                       b_raw[:, g * 4 + t, part * P:(part + 1) * P], ident[:])
                        last.then_inc(qkT_ready, 1)

                    def scores(a):
                        e, t = divmod(a, TT)
                        head, tile = slice(e * 64, e * 64 + 64), slice(t * P, (t + 1) * P)
                        if a == 0:
                            pe.wait_ge(qkT_done, h * 6 + 6)
                        if a or later:
                            pe.wait_ge(s_biased, h * 8 + a)
                        nc.tensor.matmul(score[0][:], b_qk[head, 0, tile], b_qk[head, 1, :], start=True, stop=True)
                        nc.tensor.matmul(score[1][:, 0:P], b_qk[head, 2, tile], b_qk[head, 3, tile],
                                         start=True, stop=True)
                        nc.tensor.matmul(score[1][:, P:2 * P], b_qk[head, 4, tile], b_qk[head, 5, tile],
                                         start=True, stop=True).then_inc(s_ready, 1)

                    def turn_p(a):
                        pe.wait_ge(e_done, h * 8 + (a + 1))
                        if a:
                            pe.wait_ge(pT_act, h * 8 + a)
                            pe.wait_ge(pT_dve, h * 8 + a)
                        for c in range(6):
                            last = nc.tensor.transpose(turn[c // 4][:, c % 4 * P:(c % 4 + 1) * P],
                                                       b_s[:, a % 2, c * P:(c + 1) * P], ident[:])
                        last.then_inc(pT_ready, 1)

                    def values(a):
                        e, t = divmod(a, TT)
                        pe.wait_ge(pT_act, h * 8 + (a + 1))
                        pe.wait_ge(pT_dve, h * 8 + (a + 1))
                        if a >= 2 or later:
                            pe.wait_ge(bo_done, h * 8 + (a - 1))
                        for c in range(6):
                            unit = c if c < 4 else (c - 3) * TT + t
                            last = nc.tensor.matmul((obank, spare)[a % 2][:, 0:64], b_pt[:, a % 2, c * P:(c + 1) * P],
                                                    b_v[:, prev, unit, e * 64:(e + 1) * 64],
                                                    start=(c == 0), stop=(c == 5))
                        last.then_inc(bo_ready, 1)

                    def turn_o():
                        pe.wait_ge(bo_done, h * 8 + 8)
                        for t in range(TT):
                            last = nc.tensor.transpose(turn[0][:, t * P:(t + 1) * P], b_o[:, t], ident[:])
                        last.then_inc(boT_ready, 1)

                    def bank_free(v):
                        if v in (0, 1) and not (static(i) and i == 0):
                            pe.wait_ge(u_act, i * 12 + (v - 1))
                            pe.wait_ge(u_dve, i * 12 + (v - 1))
                        elif v == 6:
                            pe.wait_ge(bgate_done, i + 1)
                        elif v >= 2:
                            u = b_unit(v - 2)
                            pe.wait_ge(u_act, i * 12 + (u + 1))
                            pe.wait_ge(u_dve, i * 12 + (u + 1))

                    steps = {}
                    if mix:
                        for b in range(6):
                            steps[QK_TURNS[b]] = [lambda b=b: turn_qk(b)]
                        for s in range(B_STEPS + 2):
                            at = steps.setdefault(SLOT + SLOT_STEP * s, [])
                            if s < B_STEPS:
                                at.append(lambda a=s: scores(a))
                            if not proj and 2 <= s < KT + 1:
                                at.append(lambda k=s - 2: wide(n, k, (0, 1)))
                            if 1 <= s <= B_STEPS:
                                at.append(lambda a=s - 1: turn_p(a))
                            if not proj and s >= B_STEPS:
                                for k in ((0, 1, 2), (3,))[s - B_STEPS]:
                                    at.append(lambda k=k: wide(n, k, (2, 3)))
                            if s >= 2:
                                at.append(lambda a=s - 2: values(a))
                        if not proj:
                            steps[100] = [lambda: wide(n, 4, (2, 3))]
                        steps[102] = [turn_o]
                        if not proj:
                            steps[102] += [lambda k=k: wide(n, k, (2, 3)) for k in (5, 6)]
                    for ks in range((B_UNITS + 1) * KT):
                        v, k = divmod(ks, KT)
                        if proj:
                            bank = acc[(par + v) % 2]
                            if k == 0:
                                if v in (0, 4, 5, 9):
                                    upto = {0: 3, 4: 4, 5: 7, 9: 10}[v]
                                    pe.wait_ge(lo_done, chunk(IN0[n], len(B_PARTS), j, par, upto))
                                bank_free(v)
                            if v == 4:
                                last = feature_step(bank[:], SLOTS - 1, k)
                            else:
                                g, t = divmod(b_unit(v), TT)
                                half = b_half(par, g) * HALF
                                last = token_step(bank[:, 0:3 * P], slice(half, half + 3), k, t)
                            if k == KT - 1:
                                last.then_inc(acc_ready, 1)
                        for step in steps.get(ks, ()):
                            step()

                iterations(pe, body)

            def layer_c(n):
                def turn_weights():
                    pe.wait_ge(cw_masked, 1)
                    pe.wait_ge(h_lo, 8 * n + 8)
                    for g in range(HEADS):
                        last = nc.tensor.transpose(turn[g // 4][:, g % 4 * P:(g % 4 + 1) * P], c_ws[:, g], ident[:])
                    last.then_inc(cwT_ready, 1)

                def spatial(g):
                    pe.wait_ge(ln_done, TT)
                    pe.wait_ge(cwT_done, 1)
                    if g >= 4:
                        pe.wait_ge(y_done, KT * n + g - 3)
                    for t in range(TT):
                        tile = ps[2 + g % 4][:, t * P:(t + 1) * P]
                        last = nc.tensor.matmul(tile, c_v[:, t, g * P:(g + 1) * P], c_wt[:, g], start=True, stop=True)
                    last.then_inc(sp_ready, 1)

                for p in range(LAYER_IN[n] // 2):
                    if p < 4:
                        pe.wait_ge(lo_done, IN0[n] + 2 * p + 2)
                        for t in range(0 if p else 2, TT):
                            v_unit(n, p, t)
                            if p == 0 and t == 2:
                                turn_weights()
                        continue
                    for c in range(2):
                        pe.wait_ge(lo_done, IN0[n] + 2 * p + c + 1)
                        if c == 0:
                            pe.wait_ge(gelu_done, 13 if p == 4 else 12 + p)
                        if c == 1 and p > 4:
                            pe.wait_ge(cgate_done, p - 4)
                        if c == 1 and p == 4:
                            pe.wait_ge(gelu_done, 14)
                        for k in range(KT):
                            last = feature_step(acc[c][:], c_ring(2 * p + c), k)
                        last.then_inc(acc_ready, 1)
                    if p >= 7:
                        spatial(p - 7)
                for g in range(5, HEADS):
                    spatial(g)
                for k in range(KT - 1):
                    wide(n, k, (0, 1))
                for k in range(KT - 1):
                    wide(n, k, (2, 3))

            for t in range(2):
                transpose_x(0, t)
            for n in range(layers):
                lead_in(n)
                if n % 3 == 0:
                    layer_a(n, n // 3)
                elif n == 1:
                    layer_b(n)
                else:
                    layer_c(n)
                output_projection(n)

        @block.scalar
        def _(act):
            def split_hi(slot, landed_at, ring):
                act.wait_ge(raw_landed[slot], landed_at)
                nc.scalar.activation(w_hi[:, ring], raw[:, slot], ACT.Copy).then_inc(hi_done, 1)

            def split_chunks(n0, per, j, par, chunks, ring):
                for c in chunks:
                    slot, at = landed(n0, per, j, par, c)
                    split_hi(slot, at, ring(par, c))

            def split_pair(n0, p):
                for c in (2 * p, 2 * p + 1):
                    split_hi((n0 + c) % RAW, 16 * ((n0 + c) // RAW + 1), c_ring(c))

            def split_out(n, chunks):
                for c in chunks:
                    at = OUT0[n] + c
                    split_hi(at % RAW, 16 * (at // RAW + 1), OUT_RING[c])

            def split_first(n, chunks):
                for c in chunks:
                    at = IN0[n] + c
                    split_hi(at % RAW, 16 * (at // RAW + 1), c)

            def square(n, t):
                if n == 0:
                    act.wait_ge(s_x[t], 16)
                else:
                    act.wait_ge(x_new, OUT_UNITS * (n - 1) + FINAL[t])
                if TT * n + t >= 2:
                    act.wait_ge(xT_done, 8 * n + 2 * t - 2)
                nc.scalar.activation(xn[:, t % 2], xt[:, t], ACT.Square,
                                     accum_out=stat[:, t:t + 1]).then_inc(ssq_done, 1)
                act.wait_ge(ssq_done, TT * n + t + 1)
                nc.scalar.activation(stat[:, 4 + t:5 + t], stat[:, t:t + 1], ACT.Sqrt, scale=1.0 / D,
                                     bias=eps[:]).then_inc(root_done, 1)

            def norm(n):
                early = n != 1
                for t in range(TT):
                    square(n, t)
                    if n == 0 and t == 2:
                        split_first(0, (0, 1))
                    if t and early:
                        h_hi_parts(n, t - 1)
                    if n == 1 and t == 2:
                        act.wait_ge(out_ready, OUT_UNITS - 1)
                        split_first(1, (2,))
                for t in range(TT - 1 if early else 0, TT):
                    h_hi_parts(n, t)

            def h_hi_parts(n, t):
                if n == 1 and t == 0:
                    act.wait_ge(out_ready, OUT_UNITS)
                for half in range(2):
                    act.wait_ge(xT_done, 8 * n + 2 * t + half + 1)
                    nc.scalar.activation(h_part(op_hi, n, t, half), turned_part(n, t, half),
                                         ACT.Copy).then_inc(h_hi, 1)

            def split_y(n, k):
                act.wait_ge(y_done, KT * n + k + 1)
                nc.scalar.activation(op_hi[:, k], y[:, k], ACT.Copy).then_inc(y_hi, 1)

            def output_chunks(n):
                act.wait_ge(out_ready, OUT_UNITS * n + WIDE)
                split_out(n, (7,))
                if n + 1 < layers:
                    split_first(n + 1, (0, 1))

            def layer_a(n, idx):
                H0, A0, per = HEADS * idx, ACC0[n], len(A_PARTS)

                def body(j, par, proj, mix, end):
                    i = j * 2 + par
                    h = i + (H0 - 1)
                    later = not static(h) or h > H0

                    if mix:
                        act.wait_ge(acc_ready, i * 4 + A0)
                        if not static(h) or h > 0:
                            act.wait_ge(gate_done, h)
                        nc.scalar.activation(a_sig[:, 1], acc[1][:], ACT.Sigmoid).then_inc(g_act, 1)
                        act.wait_ge(vT_ready, h + 1)
                        if later:
                            act.wait_ge(o_ready, h)
                        nc.scalar.activation(a_vt, turn[0][:].rearrange("p (t c) -> p t c", t=TT),
                                             ACT.Copy).then_inc(vT_done, 1)
                    if mix and not proj:
                        split_out(n, (2, 3))
                        for k in range(KT - 1):
                            split_y(n, k)
                        act.wait_ge(g_ready, h * G_STEPS + 2)
                        split_out(n, (4, 5, 6))
                    if proj:
                        if static(i) and i == 0:
                            if n:
                                act.wait_ge(out_ready, OUT_UNITS * n)
                        else:
                            act.wait_ge(acc_ready, i * 4 + A0)
                        split_chunks(IN0[n], per, j, par, (2, 3), a_ring)
                        act.wait_ge(acc_ready, i * 4 + (A0 + 1))
                        if not (static(i) and i < 2):
                            act.wait_ge(g_ready, i * G_STEPS + G_STEPS * (H0 - 1))
                        if not (static(i) and i + H0 == 0):
                            act.wait_ge(kf_done, i + H0)
                        nc.scalar.activation(a_t[:, par, 0:S], acc[0][:], ACT.Sigmoid)
                        nc.scalar.activation(a_sig[:, 2], acc[0][:], ACT.Sigmoid, scale=-1.0).then_inc(f_act, 1)
                        act.wait_ge(acc_ready, i * 4 + (A0 + 2))
                        if not (static(i) and i + H0 == 0):
                            act.wait_ge(q_done, i + H0)
                        nc.scalar.activation(a_sig[:, 0], acc[1][:], ACT.Sigmoid).then_inc(q_act, 1)
                        split_chunks(IN0[n], per, j if par == 0 else j + 1, 1 - par, (0, 1), a_ring)
                        act.wait_ge(qk_done, i + (H0 + 1))
                        if not (static(i) and i < 1):
                            act.wait_ge(g_ready, i * G_STEPS + (G_STEPS * (H0 - 1) + 2))
                        nc.scalar.activation(qk_hi, a_qk, ACT.Copy).then_inc(qk_hi_done, 1)
                    if mix:
                        act.wait_ge(g_ready, h * G_STEPS + (LEVELS + 2))
                        if later:
                            act.wait_ge(o_ready, h)
                        nc.scalar.activation(a_sx[:, 0:2], score[0][:, 0:256].rearrange("p (t c) -> p t c", t=2),
                                             ACT.Copy).then_inc(sx_done, 1)
                        act.wait_ge(g_ready, h * G_STEPS + (LEVELS + 3))
                        nc.scalar.activation(a_sx[:, 2:6], score[1][:].rearrange("p (t c) -> p t c", t=4),
                                             ACT.Copy).then_inc(sx_done, 1)
                    if proj:
                        act.wait_ge(acc_ready, i * 4 + (A0 + 3))
                        if not (static(i) and i < 2):
                            act.wait_ge(vT_ready, i + (H0 - 1))
                        nc.scalar.activation(a_v[:, par], acc[0][:], ACT.Copy).then_inc(v_act, 1)
                    if mix:
                        act.wait_ge(o_ready, h + 1)
                        if not static(h) or h > 0:
                            act.wait_ge(oms_done, h)
                        nc.scalar.activation(a_sq, obank[:].rearrange("p (t c) -> p t c", t=TT),
                                             ACT.Square).then_inc(sq_done, 1)
                        act.wait_ge(oms_done, h + 1)
                        if not static(h) or h > 0:
                            act.wait_ge(rs_done, h)
                        nc.scalar.activation(a_ss[:, 1], a_ss[:, 0], ACT.Sqrt, scale=1.0 / P,
                                             bias=eps[:]).then_inc(oroot_done, 1)

                iterations(act, body)

            def layer_b(n):
                B0, per = ACC0[n], len(B_PARTS)

                def body(j, par, proj, mix, end):
                    i = j * 2 + par
                    h = i - 1
                    later = not static(h) or h > 0
                    prev = 1 - par

                    def qk_out(b):
                        act.wait_ge(qkT_ready, h * 6 + (b + 1))
                        if later:
                            act.wait_ge(s_ready, h * 8)
                        g, part = divmod(b, 2)
                        col = 18 + 3 * part + g
                        nc.scalar.activation(b_qk[:, b], turn[b % 2][:], ACT.Copy,
                                             scale=vec[:, col:col + 1]).then_inc(qkT_done, 1)

                    def exps(a):
                        act.wait_ge(m_done, h * 8 + (a + 1))
                        if a >= 2 or later:
                            act.wait_ge(l_done, h * 8 + (a - 1))
                        nc.scalar.activation(b_s[:, a % 2], b_s[:, a % 2], ACT.Exp, bias=b_small[:, 0, a % 2:a % 2 + 1],
                                             accum_out=b_small[:, 1, a % 2:a % 2 + 1]).then_inc(e_done, 1)

                    def p_out(a):
                        act.wait_ge(pT_ready, h * 8 + (a + 1))
                        if a >= 2 or later:
                            act.wait_ge(bo_ready, h * 8 + (a - 1))
                        nc.scalar.activation(b_pt[:, a % 2, 0:S], turn[0][:], ACT.Copy).then_inc(pT_act, 1)

                    def unit(v):
                        u = b_unit(v)
                        bank = acc[(par + v) % 2]
                        act.wait_ge(acc_ready, i * 13 + (B0 + v + 1))
                        if not (static(i) and i == 0 and u == 0):
                            act.wait_ge(u_dve, i * 12 + u)
                        nc.scalar.activation(b_sq, bank[:, 0:256], ACT.Square)
                        if u == 0 and not (static(i) and i < 2):
                            act.wait_ge(bo_ready, i * 8 - 8)
                        nc.scalar.activation(b_v[:, par, u], bank[:, 256:384], ACT.Copy).then_inc(u_act, 1)

                    def gate():
                        act.wait_ge(acc_ready, i * 13 + (B0 + 5))
                        if not (static(i) and i == 0):
                            act.wait_ge(bgate_done, i)
                        nc.scalar.activation(b_eg, acc[par][:], ACT.Exp, scale=-1.0).then_inc(eg_done, 1)

                    def roots():
                        act.wait_ge(u_dve, i * 12 + 12)
                        if not (static(i) and i == 0):
                            act.wait_ge(qn_done, i * 3)
                        nc.scalar.activation(b_rs, b_ss, ACT.Sqrt, scale=1.0 / 64, bias=eps[:]).then_inc(broot_done, 1)

                    def chunks(cs, used, value):
                        act.wait_ge(used, value)
                        split_chunks(IN0[n], per, j, par, cs, b_ring)

                    def next_group0():
                        act.wait_ge(acc_ready, i * 13 + (B0 + 9))
                        if static(i) and i == HEADS - 1:
                            split_out(n, (0, 1))
                        else:
                            split_chunks(IN0[n], per, j if par == 0 else j + 1, 1 - par, (0, 1, 2), b_ring)

                    plan = []
                    if proj:
                        first = static(i) and i == 0
                        if first:
                            plan.append((1, lambda: chunks((3, 4, 5, 6), out_ready, OUT_UNITS)))
                        else:
                            plan.append((1, lambda: chunks((3, 4, 5), acc_ready, i * 13 + B0)))
                            plan.append((SLOT + 6.5, lambda: chunks((6,), acc_ready, i * 13 + B0)))
                        plan.append((33, lambda: chunks((7, 8, 9), acc_ready, i * 13 + (B0 + 4))))
                        plan.append((73, next_group0))
                        for v in range(B_UNITS + 1):
                            plan.append((8 * v + 8, gate if v == 4 else lambda v=v: unit(v)))
                        plan.append((104.5, roots))
                    if mix:
                        for b in range(6):
                            plan.append((QK_TURNS[b] + 1, lambda b=b: qk_out(b)))
                        for a in range(B_STEPS):
                            plan.append((SLOT + SLOT_STEP * a + 4, lambda a=a: exps(a)))
                            plan.append((SLOT + SLOT_STEP * a + 10.5, lambda a=a: p_out(a)))
                    if mix and not proj:
                        plan.append((1, lambda: act.wait_ge(acc_ready, B0 + ACC_OF[n])))
                        plan.append((1.1, lambda: split_out(n, (2, 3))))
                        for k in range(KT - 1):
                            plan.append((SLOT + SLOT_STEP * k + 3.5, lambda k=k: split_y(n, k)))
                        for c in (4, 5, 6):
                            plan.append((SLOT + SLOT_STEP * c - 10, lambda c=c: split_out(n, (c,))))
                    for _, step in sorted(plan, key=lambda p: p[0]):
                        step()

                iterations(act, body, peeled=1)

            def layer_c(n):
                C0 = ACC0[n]

                def weights_out():
                    act.wait_ge(cwT_ready, 1)
                    for half in range(2):
                        last = nc.scalar.activation(c_wt[:, half * 4:half * 4 + 4],
                                                    turn[half][:].rearrange("p (g c) -> p g c", g=4), ACT.Copy)
                    last.then_inc(cwT_done, 1)

                def gelu(u, bank, width):
                    if u >= 2:
                        act.wait_ge(z_done, u - 1)
                    nc.scalar.activation(c_x2[:, u % 2, 0:width], bank, ACT.Square).then_inc(sqc_done, 1)
                    act.wait_ge(z_done, u + 1)
                    nc.scalar.activation(c_z[:, u % 2, 0:width], c_z[:, u % 2, 0:width], ACT.Sigmoid,
                                         scale=GELU_SCALE).then_inc(sig_done, 1)

                for p in range(LAYER_IN[n] // 2):
                    def next_pair():
                        before = C0 + (4 * p if p <= 4 else 16 + 2 * (p - 4))
                        if p == 0:
                            act.wait_ge(out_ready, OUT_UNITS * n)
                        else:
                            act.wait_ge(acc_ready, before)
                        if p + 1 < LAYER_IN[n] // 2:
                            split_pair(IN0[n], p + 1)
                        else:
                            split_out(n, (0, 1, 2, 3))
                    next_pair()
                    if p < 4:
                        for t in range(TT):
                            u = 4 * p + t
                            act.wait_ge(acc_ready, C0 + u + 1)
                            gelu(u, v_bank(u), 256)
                            if u == 1:
                                weights_out()
                        continue
                    if p == 4:
                        for t in range(TT):
                            act.wait_ge(cms_done, t + 1)
                            nc.scalar.activation(c_mv[:, t, 2:3], c_mv[:, t, 1:2], ACT.Sqrt,
                                                 bias=eps[:]).then_inc(croot_done, 1)
                    g = p - 4
                    act.wait_ge(acc_ready, C0 + 16 + 2 * g + 1)
                    gelu(16 + g, acc[0][:], S)
                    act.wait_ge(acc_ready, C0 + 16 + 2 * g + 2)
                    if g >= 1:
                        act.wait_ge(cgate_done, g)
                    nc.scalar.activation(c_g[:, 0], acc[1][:], ACT.Sigmoid).then_inc(cg_act, 1)
                for k in range(4):
                    split_y(n, k)
                split_out(n, (4, 5, 6))
                for k in range(4, KT - 1):
                    split_y(n, k)

            act.wait_ge(s_set, 1)
            nc.scalar.activation(stat[:, 15:16], eps[:], ACT.Sqrt)
            norm(0)
            act.wait_ge(bound_step, 1)
            nc.scalar.activation(bound[:, 2], bound[:, 2], ACT.Exp).then_inc(s_bact, 1)
            for n in range(layers):
                if n:
                    norm(n)
                if n % 3 == 0:
                    layer_a(n, n // 3)
                elif n == 1:
                    layer_b(n)
                else:
                    layer_c(n)
                split_y(n, KT - 1)
                output_chunks(n)

        @block.vector
        def _(dve):
            def scale(n, t):
                dve.wait_ge(root_done, TT * n + t + 1)
                nc.vector.reciprocal(stat[:, 8 + t:9 + t], stat[:, 4 + t:5 + t]).then_inc(rstd_done, 1)
                dve.wait_ge(rstd_done, TT * n + t + 1)
                if t == 0:
                    dve.wait_ge(s_normw, 16 * (n + 1))
                for half in range(2):
                    cols = slice(half * 512, (half + 1) * 512)
                    nc.vector.scalar_tensor_tensor(xn[:, t % 2, cols], xt[:, t, cols], stat[:, 8 + t:9 + t],
                                                   norm_b[:, cols], ALU.mult, ALU.mult).then_inc(xn_done, 1)

            def first_norm():
                for t in range(TT):
                    scale(0, t)
                    if t:
                        h_lo_parts(0, t - 1)
                h_lo_parts(0, TT - 1)

            def h_lo_parts(n, t):
                for half in range(2):
                    dve.wait_ge(h_hi, 8 * n + 2 * t + half + 1)
                    nc.vector.tensor_tensor(h_part(op_lo, n, t, half), turned_part(n, t, half),
                                            h_part(op_hi, n, t, half).bitcast(F32), ALU.subtract).then_inc(h_lo, 1)

            def split_y(n, k):
                dve.wait_ge(y_hi, KT * n + k + 1)
                nc.vector.tensor_tensor(op_lo[:, k], y[:, k], op_hi[:, k].bitcast(F32),
                                        ALU.subtract).then_inc(y_lo, 1)

            def residual(n):
                def add(u):
                    if u < WIDE:
                        t, cols, of = u, slice(0, 512), wide_bank(n, u)[:]
                    else:
                        b, t = NARROW[u - WIDE]
                        cols, of = slice(512 + b * 256, 768 + b * 256), acc[u % 2][:, 0:256]
                    dve.wait_ge(out_ready, OUT_UNITS * n + u + 1)
                    nc.vector.tensor_tensor(xt[:, t, cols], xt[:, t, cols], of, ALU.add).then_inc(x_new, 1)

                early = n > 0
                for u in range(OUT_UNITS):
                    add(u)
                    if n + 1 < layers and u in (7, 8, 9, 11):
                        t = (7, 8, 9, 11).index(u)
                        scale(n + 1, t)
                        if t and early:
                            h_lo_parts(n + 1, t - 1)
                if n + 1 < layers:
                    for t in range(TT - 1 if early else 0, TT):
                        h_lo_parts(n + 1, t)

            def bounds():
                steps = [0]

                def step(ins):
                    steps[0] += 1
                    ins.then_inc(bound_step, 1)
                    dve.wait_ge(bound_step, steps[0])

                dve.wait_ge(s_vecT, 1)
                nc.vector.tensor_copy(vec[:], spare[:, 0:24]).then_inc(vec_step, 1)
                dve.wait_ge(vec_step, 1)
                l0, l1 = vec[:, 0:8], vec[:, 8:16]
                b = [bound[:, c, l] for c in range(5) for l in range(2)]
                nc.vector.tensor_scalar(vec[:, 18:21], vec[:, 18:21], 64 ** -0.5, None, ALU.mult)
                nc.vector.tensor_tensor(b[8], l0, l1, ALU.max).then_inc(vec_step, 1)
                dve.wait_ge(vec_step, 2)
                nc.vector.tensor_tensor(b[4], l0, b[8], ALU.subtract)
                step(nc.vector.tensor_tensor(b[5], l1, b[8], ALU.subtract))
                dve.wait_ge(s_bact, 1)
                step(nc.vector.tensor_tensor(b[8], b[4], b[5], ALU.add))
                step(nc.vector.reciprocal(b[9], b[8]))
                nc.vector.tensor_tensor(b[6], b[4], b[9], ALU.mult)
                step(nc.vector.tensor_tensor(b[7], b[5], b[9], ALU.mult))
                step(nc.vector.tensor_tensor(b[5], b[6], b[7], ALU.add))
                nc.vector.tensor_tensor(b[4], b[6], b[6], ALU.subtract)
                step(nc.vector.tensor_tensor(b[5], b[5], b[6], ALU.subtract))
                nc.vector.tensor_scalar(bound[:, 0], bound[:, 2], LB_FLOOR, None, ALU.max)
                step(nc.vector.tensor_scalar(bound[:, 1], bound[:, 2], -1.0, 1.0, ALU.mult, ALU.add))

            def layer_a(n, idx):
                H0 = HEADS * idx
                if n == 0:
                    dve.wait_ge(s_mask, 16)
                    nc.vector.tensor_copy(a_mask[:], mask_f)
                nc.vector.memset(a_sq[:, 0], 1.0)
                nc.vector.memset(a_sd, 0.0).then_inc(sd_zero, 1)
                dve.wait_ge(sd_zero, idx + 1)
                nc.vector.tensor_copy(ones_sq, a_sq[:, 0])

                def body(j, par, proj, mix, end):
                    i = j * 2 + par
                    h = i + (H0 - 1)
                    prev = 1 - par
                    later = not static(h) or h > H0

                    def gate():
                        dve.wait_ge(g_act, h + 1)
                        nc.vector.tensor_tensor(a_gate[:, prev], acc[1][:], a_sig[:, 1],
                                                ALU.mult).then_inc(gate_done, 1)

                    def forget():
                        dve.wait_ge(f_act, i + (H0 + 1))
                        one_minus, floor = bound[:, 1, idx, bass.ds(i, 1)], bound[:, 0, idx, bass.ds(i, 1)]
                        nc.vector.tensor_scalar(a_t[:, par, 0:S], a_t[:, par, 0:S], one_minus, floor, ALU.mult, ALU.add)
                        nc.vector.tensor_scalar(a_k[:, par], a_sig[:, 2], one_minus, None,
                                                ALU.mult).then_inc(kf_done, 1)
                        dve.wait_ge(kf_done, i + (H0 + 1))

                    def decays(which):
                        for s in which:
                            size = S >> s
                            at = 2 * S - 2 * size
                            pairs = a_t[:, par, at:at + size].rearrange("p (b u) -> p b u", u=2)
                            nc.vector.tensor_tensor(a_t[:, par, at + size:at + size + size // 2],
                                                    pairs[:, :, 0], pairs[:, :, 1], ALU.mult).then_inc(t_step, 1)
                            dve.wait_ge(t_step, i * LEVELS + (LEVELS * H0 + s + 1))

                    def query():
                        dve.wait_ge(q_act, i + (H0 + 1))
                        nc.vector.tensor_tensor(a_q[:, par], acc[1][:], a_sig[:, 0], ALU.mult).then_inc(q_done, 1)

                    def products():
                        q, k = a_q[:, par], a_k[:, par]
                        dve.wait_ge(q_done, i + (H0 + 1))
                        if not (static(i) and i + H0 == 0):
                            dve.wait_ge(qk_lo_done, i + H0)
                        nc.vector.tensor_tensor(a_qk[:, 0:S], q, k, ALU.mult)
                        nc.vector.tensor_tensor(q, q, a_t[:, par, 0:S], ALU.mult).then_inc(qf_done, 1)

                    def pair_products():
                        q, k = a_q[:, par], a_k[:, par]
                        dve.wait_ge(qf_done, i + (H0 + 1))
                        nc.vector.tensor_tensor(a_qk[:, S:], q.rearrange("p (b u) -> p b u", u=2)[:, :, 1],
                                                k.rearrange("p (b u) -> p b u", u=2)[:, :, 0],
                                                ALU.mult).then_inc(qk_done, 1)

                    def split_products():
                        dve.wait_ge(qk_hi_done, i + (H0 + 1))
                        nc.vector.tensor_tensor(qk_lo, a_qk, qk_hi.bitcast(F32), ALU.subtract).then_inc(qk_lo_done, 1)

                    def taken(g):
                        dve.wait_ge(g_ready, h * G_STEPS + (g + 1))
                        if 0 < g < 8:
                            dve.wait_ge(sd_done, h * 8 + g)
                        elif g == 0 and later:
                            dve.wait_ge(o_ready, h)

                    def move_on(g):
                        m = 1 << (g - 1)
                        nb = S // (2 * m)
                        start = 2 * S - 2 * S // m
                        decay = a_t[:, prev, start:start + 2 * nb].rearrange("p (b u) -> p b u", u=2)
                        q = a_q[:, prev].rearrange("p (b u m) -> p b u m", u=2, m=m)[:, :, 1, :]
                        k = a_k[:, prev].rearrange("p (b u m) -> p b u m", u=2, m=m)[:, :, 0, :]
                        nc.vector.tensor_tensor(q, q, decay[:, :, 0].unsqueeze(2).to_broadcast([P, nb, m]), ALU.mult)
                        nc.vector.tensor_tensor(k, k, decay[:, :, 1].unsqueeze(2).to_broadcast([P, nb, m]),
                                                ALU.mult).then_inc(upd, 1)

                    def keep(g):
                        if g == 0:
                            ins = nc.vector.copy_predicated(a_sd.rearrange("p t c -> p (t c)"), a_mask[:, 0:S],
                                                            score[0][:])
                        else:
                            m = 1 << (g - 1)
                            to = a_sd.rearrange("p t (b u m) -> p (t b) u m", u=2, m=m)[:, :, 1, :]
                            mask = a_mask[:, S + (g - 1) * 256:S + g * 256].rearrange("p (b m) -> p b m", m=m)
                            of = score[g % 2][:, 0:256].rearrange("p (b m) -> p b m", m=m)
                            ins = nc.vector.copy_predicated(to, mask, of)
                        ins.then_inc(sd_done, 1)

                    def o_norm():
                        dve.wait_ge(sq_done, h + 1)
                        nc.vector.tensor_reduce(a_ss[:, 0], a_sq, AX, ALU.add).then_inc(oms_done, 1)
                        dve.wait_ge(oroot_done, h + 1)
                        nc.vector.reciprocal(a_ss[:, 2], a_ss[:, 1]).then_inc(rs_done, 1)
                        dve.wait_ge(rs_done, h + 1)
                        if later:
                            dve.wait_ge(oT_ready, h)
                        nc.vector.tensor_tensor(a_on, obank[:].rearrange("p (t c) -> p t c", t=TT),
                                                a_ss[:, 2].unsqueeze(2).to_broadcast([P, TT, P]),
                                                ALU.mult).then_inc(on_done, 1)

                    def into_y():
                        dve.wait_ge(oT_ready, h)
                        nc.vector.scalar_tensor_tensor(y[:, i - 2], turn[1][:], vec[:, 16 + idx:17 + idx],
                                                       a_gate[:, par], ALU.mult, ALU.mult).then_inc(y_done, 1)

                    for g in range(8):
                        if mix:
                            taken(g)
                            gate() if g == 0 else move_on(g)
                            keep(g)
                        if mix and not proj and g > 1:
                            split_y(n, g - 2)
                        if g == 0 and end:
                            into_y()
                        if g == 3 and proj:
                            forget()
                        if g == 6 and proj:
                            query()
                        if g == 7 and proj:
                            products()
                        if g >= 4 and proj:
                            decays({4: (0,), 5: (1, 2), 6: (3, 4), 7: (5, 6)}[g])
                    if mix:
                        taken(8)
                        move_on(8)
                    if mix and not proj:
                        split_y(n, 6)
                    if proj:
                        pair_products()
                        split_products()
                    if mix:
                        o_norm()

                iterations(dve, body)

            def layer_b(n):
                dve.wait_ge(s_dist, 16)

                def body(j, par, proj, mix, end):
                    i = j * 2 + par
                    h = i - 1
                    prev = 1 - par
                    later = not static(h) or h > 0

                    def unit(v):
                        u = b_unit(v)
                        bank = acc[(par + v) % 2]
                        dve.wait_ge(u_act, i * 12 + (u + 1))
                        if mix and u % 4 == 0:
                            dve.wait_ge(qkT_ready, h * 6 + (2 * (u // 4) + 2))
                        nc.vector.tensor_copy(b_raw[:, u], bank[:, 0:256])
                        if u == 0 and not (static(i) and i == 0):
                            dve.wait_ge(broot_done, i)
                        nc.vector.tensor_reduce(b_ss[:, u * 4:u * 4 + 4], b_sq.rearrange("p (c d) -> p c d", c=4),
                                                AX, ALU.add).then_inc(u_dve, 1)

                    def gate():
                        dve.wait_ge(eg_done, i + 1)
                        nc.vector.tensor_scalar(b_eg, b_eg, 1.0, None, ALU.add).then_inc(bg_step, 1)
                        dve.wait_ge(bg_step, i * 2 + 1)
                        nc.vector.reciprocal(b_eg, b_eg).then_inc(bg_step, 1)
                        dve.wait_ge(bg_step, i * 2 + 2)
                        nc.vector.tensor_tensor(b_gate[:, par], acc[par][:], b_eg, ALU.mult).then_inc(bgate_done, 1)

                    def norm_qk():
                        dve.wait_ge(broot_done, h + 1)
                        nc.vector.reciprocal(b_rs, b_rs).then_inc(brs_done, 1)
                        dve.wait_ge(brs_done, h + 1)
                        for g in range(3):
                            q = b_raw[:, g * 4:g * 4 + 4].rearrange("p t (c d) -> p (t c) d", c=4)
                            r = b_rs[:, g * 16:g * 16 + 16].unsqueeze(2).to_broadcast([P, 16, 64])
                            nc.vector.tensor_tensor(q, q, r, ALU.mult).then_inc(qn_done, 1)

                    def bias(a):
                        e, t = divmod(a, TT)
                        dve.wait_ge(s_ready, h * 8 + (a + 1))
                        if a >= 2 or later:
                            dve.wait_ge(pT_ready, h * 8 + (a - 1))
                        parts = ((slice(0, S), b_dist[:, t * S:(t + 1) * S], score[0][:]),
                                 (slice(S, S + P), b_dist[:, TT * S:TT * S + P], score[1][:, 0:P]),
                                 (slice(S + P, S + 2 * P), b_dist[:, TT * S + P:], score[1][:, P:2 * P]))
                        for g, (to, dist, of) in enumerate(parts):
                            last = nc.vector.scalar_tensor_tensor(b_s[:, a % 2, to], dist,
                                                                  slope[:, bass.ds(h * 2 + (16 * g + e), 1)], of,
                                                                  ALU.mult, ALU.add)
                        last.then_inc(s_biased, 1)
                        dve.wait_ge(s_biased, h * 8 + (a + 1))
                        nc.vector.tensor_reduce(b_small[:, 0, a % 2:a % 2 + 1], b_s[:, a % 2], AX, ALU.max,
                                                negate=True).then_inc(m_done, 1)

                    def p_out(a):
                        dve.wait_ge(pT_ready, h * 8 + (a + 1))
                        if a >= 2 or later:
                            dve.wait_ge(bo_ready, h * 8 + (a - 1))
                        nc.vector.tensor_copy(b_pt[:, a % 2, S:], turn[1][:, 0:256]).then_inc(pT_dve, 1)

                    def o_out(a):
                        e, t = divmod(a, TT)
                        dve.wait_ge(e_done, h * 8 + (a + 1))
                        nc.vector.reciprocal(b_small[:, 2, a % 2:a % 2 + 1],
                                             b_small[:, 1, a % 2:a % 2 + 1]).then_inc(l_done, 1)
                        dve.wait_ge(l_done, h * 8 + (a + 1))
                        dve.wait_ge(bo_ready, h * 8 + (a + 1))
                        if a == 0 and later:
                            dve.wait_ge(boT_ready, h)
                        nc.vector.tensor_scalar(b_o[:, t, e * 64:(e + 1) * 64], (obank, spare)[a % 2][:, 0:64],
                                                b_small[:, 2, a % 2:a % 2 + 1], None, ALU.mult).then_inc(bo_done, 1)

                    def into_y():
                        dve.wait_ge(boT_ready, h + 1)
                        split = "p (r q a) -> p r q a"
                        nc.vector.tensor_tensor(y[:, h].rearrange("p (a q r) -> p r q a", q=4, r=4),
                                                turn[0][:].rearrange(split, r=4, q=4),
                                                b_gate[:, prev].rearrange(split, r=4, q=4),
                                                ALU.mult).then_inc(y_done, 1)

                    plan = []
                    if proj:
                        for v in range(B_UNITS + 1):
                            plan.append((8 * v + 8.5, gate if v == 4 else lambda v=v: unit(v)))
                    if mix:
                        plan.append((0, norm_qk))
                        for a in range(B_STEPS):
                            plan.append((SLOT + SLOT_STEP * a + 0.5, lambda a=a: bias(a)))
                            plan.append((SLOT + SLOT_STEP * a + 10.4, lambda a=a: p_out(a)))
                            plan.append((SLOT + SLOT_STEP * a + 19, lambda a=a: o_out(a)))
                        plan.append((103.5, into_y))
                    if mix and not proj:
                        for k in range(KT - 1):
                            plan.append((SLOT + SLOT_STEP * k + 0.6, lambda k=k: split_y(n, k)))
                    for _, step in sorted(plan, key=lambda p: p[0]):
                        step()

                iterations(dve, body)

            def layer_c(n):
                dve.wait_ge(s_cvec, 80)
                nc.vector.tensor_tensor(c_ws, c_ws, causal.unsqueeze(1).to_broadcast([P, HEADS, P]),
                                        ALU.mult).then_inc(cw_masked, 1)

                def gelu(u, bank, width, to):
                    dve.wait_ge(sqc_done, u + 1)
                    if u >= 2:
                        dve.wait_ge(gelu_done, u - 1)
                    z = c_z[:, u % 2, 0:width]
                    nc.vector.tensor_scalar(z, c_x2[:, u % 2, 0:width], 0.044715, 1.0,
                                            ALU.mult, ALU.add).then_inc(poly_done, 1)
                    dve.wait_ge(poly_done, u + 1)
                    nc.vector.tensor_tensor(z, z, bank, ALU.mult).then_inc(z_done, 1)
                    dve.wait_ge(sig_done, u + 1)
                    nc.vector.tensor_tensor(to, z, bank, ALU.mult).then_inc(gelu_done, 1)

                def statistics():
                    for t in range(TT):
                        for half in range(2):
                            last = nc.vector.bn_stats(c_st[:, t, half * 6:half * 6 + 6],
                                                      c_v[:, t, half * 512:(half + 1) * 512])
                        last.then_inc(cstat_done, 1)
                        dve.wait_ge(cstat_done, t + 1)
                        nc.vector.bn_aggr(c_mv[:, t, 0:2], c_st[:, t]).then_inc(cms_done, 1)

                def layer_norm(ts):
                    for t in ts:
                        dve.wait_ge(croot_done, t + 1)
                        nc.vector.reciprocal(c_mv[:, t, 3:4], c_mv[:, t, 2:3]).then_inc(ln_step, 1)
                        dve.wait_ge(ln_step, 3 * t + 1)
                        nc.vector.tensor_scalar(c_v[:, t], c_v[:, t], c_mv[:, t, 0:1], c_mv[:, t, 3:4],
                                                ALU.subtract, ALU.mult).then_inc(ln_step, 1)
                        dve.wait_ge(ln_step, 3 * t + 2)
                        nc.vector.tensor_tensor(c_v[:, t], c_v[:, t], c_vw, ALU.mult).then_inc(ln_step, 1)
                        dve.wait_ge(ln_step, 3 * t + 3)
                        nc.vector.tensor_tensor(c_v[:, t], c_v[:, t], c_vb, ALU.add).then_inc(ln_done, 1)

                def gated(g):
                    dve.wait_ge(sp_ready, g + 1)
                    if g:
                        dve.wait_ge(y_done, KT * n + g)
                    nc.vector.tensor_tensor(c_sp.rearrange("p (t c) -> p t c", t=TT),
                                            ps[2 + g % 4][:].rearrange("p (t c) -> p t c", t=TT),
                                            c_bs[:, g].unsqueeze(1).to_broadcast([P, TT, P]),
                                            ALU.add).then_inc(sp_done, 1)
                    dve.wait_ge(sp_done, g + 1)
                    nc.vector.tensor_tensor(y[:, g], y[:, g], c_sp, ALU.mult).then_inc(y_done, 1)

                for u in range(16):
                    p, t = divmod(u, TT)
                    gelu(u, v_bank(u), 256, c_v[:, t, p * 256:(p + 1) * 256])
                dve.wait_ge(gelu_done, 16)
                statistics()
                for g in range(HEADS):
                    layer_norm({1: (0,), 2: (1, 2), 3: (3,)}.get(g, ()))
                    gelu(16 + g, acc[0][:], S, y[:, g])
                    dve.wait_ge(cg_act, g + 1)
                    nc.vector.tensor_tensor(c_g[:, 1], c_g[:, 0], acc[1][:], ALU.mult).then_inc(cgate_done, 1)
                    dve.wait_ge(cgate_done, g + 1)
                    nc.vector.tensor_tensor(y[:, g], y[:, g], c_g[:, 1], ALU.mult).then_inc(cug_done, 1)
                    dve.wait_ge(cug_done, g + 1)
                    if g == HEADS - 1:
                        for k in (0, 1):
                            split_y(n, k)
                    if g >= 3:
                        gated(g - 3)
                for g, k in ((5, 2), (6, 3), (7, 4)):
                    split_y(n, k)
                    gated(g)
                for k in (5, 6):
                    split_y(n, k)

            nc.vector.memset(eps[:], EPS).then_inc(s_set, 1)
            first_norm()
            bounds()
            for n in range(layers):
                if n % 3 == 0:
                    layer_a(n, n // 3)
                elif n == 1:
                    layer_b(n)
                else:
                    layer_c(n)
                split_y(n, KT - 1)
                residual(n)


_INPUTS = ("x", "norm_w", "a_w_in", "a_lower_bounds", "a_o_norm_w", "a_w_out", "b_w_in", "b_q_norm_w",
           "b_k_norm_w", "b_w_out", "c_w_in", "c_v_norm_w", "c_v_norm_b", "c_w_s", "c_b_s", "c_w_out")


def kernel(**inputs):
    import concourse.bacc as bacc
    from concourse.bass_utils import run_bass_kernel_spmd

    nc = bacc.Bacc("TRN2", target_bir_lowering=False, num_devices=1)
    arrays = {f"in_{name}": np.ascontiguousarray(inputs[name]) for name in _INPUTS}
    arrays.update(shape_constants())
    args = [nc.dram_tensor(name, a.shape, mybir.dt.from_np(a.dtype), kind="ExternalInput").ap()
            for name, a in arrays.items()]
    result = nc.dram_tensor("out_0", (1, S, D), F32, kind="ExternalOutput").ap()
    build(nc, *args, result)
    r = run_bass_kernel_spmd(nc, [arrays], core_ids=[0])
    return r.results[0]["out_0"]
```
